# Optimizing a Trainium2 kernel written in Bass

```python
import math
import jax, jax.numpy as jnp
from jax import lax
import numpy as np

D_MODEL = 1024
BATCH = 1
SEQ = 1024
DEPTH = 1

D_MIX = D_MODEL
RWKV_WIDTH = D_MIX // 2
RWKV_HEAD = 64
RWKV_HEADS = RWKV_WIDTH // RWKV_HEAD
DECAY_LORA = 64
ICLR_LORA = 64
RWKV_GN_EPS = 64e-5
DIFF_WIDTH = D_MIX - RWKV_WIDTH
DIFF_HEAD_V = 128
DIFF_HEAD_QK = DIFF_HEAD_V // 2
DIFF_HEADS = DIFF_WIDTH // DIFF_HEAD_V
DIFF_QK_WIDTH = DIFF_HEADS * 2 * DIFF_HEAD_QK
Q_BLOCK = 128
NORM_EPS = 1e-6
QK_NORM_EPS = 1e-6
SUBLN_EPS = 1e-5
NEG_INF = -1e30

SHIFT_COLS = 3 * RWKV_WIDTH + DECAY_LORA + ICLR_LORA
SHIFT_SPLIT = (RWKV_WIDTH, 2 * RWKV_WIDTH, 3 * RWKV_WIDTH, 3 * RWKV_WIDTH + DECAY_LORA)
REST_SPLIT = (RWKV_WIDTH, RWKV_WIDTH + DIFF_QK_WIDTH, RWKV_WIDTH + 2 * DIFF_QK_WIDTH,
              RWKV_WIDTH + 2 * DIFF_QK_WIDTH + DIFF_WIDTH)
IN_COLS = SHIFT_COLS + RWKV_WIDTH + 2 * DIFF_QK_WIDTH + 2 * DIFF_WIDTH

kernel_name = "hymba_rwkv7_diffattn_alibi_block"

def rms_norm(x, g, eps):
    xf = x.astype(jnp.float32)
    y = xf * lax.rsqrt(jnp.mean(xf * xf, axis=-1, keepdims=True) + eps)
    return (y * g.astype(jnp.float32)).astype(x.dtype)

def token_shift(p, mu):
    prev = jnp.pad(p, ((0, 0), (1, 0), (0, 0)))[:, :-1]
    return p + (prev - p) * mu

def alibi_slopes(n):
    return jnp.asarray([2.0 ** (-8.0 * (h + 1) / n) for h in range(n)], jnp.float32)

def rwkv7_recurrence(r, w, k, v, a, b):
    B, T, H, N = r.shape

    def step(S, inp):
        r_t, w_t, k_t, v_t, a_t, b_t = inp
        sa = jnp.einsum('bhij,bhj->bhi', S, a_t)
        S = S * w_t[:, :, None, :] + sa[..., None] * b_t[:, :, None, :] + v_t[..., None] * k_t[:, :, None, :]
        y = jnp.einsum('bhij,bhj->bhi', S, r_t)
        return S, y

    xs = tuple(jnp.moveaxis(t, 1, 0) for t in (r, w, k, v, a, b))
    S0 = jnp.zeros((B, H, N, N), jnp.float32)
    _, y = lax.scan(step, S0, xs)
    return jnp.moveaxis(y, 0, 1)

def rwkv7_branch(r, k, v, zw, za, w0, w_decay_up, a0, w_iclr_up, k_k, k_a, r_k, ln_w, ln_b):
    B, T, _ = r.shape
    f32 = jnp.float32
    hn = (RWKV_HEADS, RWKV_HEAD)
    heads = lambda t: t.astype(f32).reshape(B, T, RWKV_HEADS, RWKV_HEAD)
    w = -jax.nn.softplus(-(w0.astype(f32) + jnp.tanh(zw.astype(f32)) @ w_decay_up.astype(f32))) - 0.5
    decay = jnp.exp(-jnp.exp(w))
    a = jax.nn.sigmoid(a0.astype(f32) + za.astype(f32) @ w_iclr_up.astype(f32))
    r, k, v, decay, a = heads(r), heads(k), heads(v), heads(decay), heads(a)
    kk = k * k_k.astype(f32).reshape(hn)
    kk = kk / jnp.maximum(jnp.sqrt(jnp.sum(kk * kk, axis=-1, keepdims=True)), 1e-12)
    k = k * (1.0 + (a - 1.0) * k_a.astype(f32).reshape(hn))
    y = rwkv7_recurrence(r, decay, k, v, -kk, kk * a)
    mu = jnp.mean(y, axis=-1, keepdims=True)
    var = jnp.mean(jnp.square(y - mu), axis=-1, keepdims=True)
    y = (y - mu) * lax.rsqrt(var + RWKV_GN_EPS) * ln_w.astype(f32).reshape(hn) + ln_b.astype(f32).reshape(hn)
    y = y + jnp.sum(r * k * r_k.astype(f32), axis=-1, keepdims=True) * v
    return y.reshape(B, T, RWKV_WIDTH)

def diff_attention_branch(q, k, v, q_norm_g, k_norm_g, lq1, lk1, lq2, lk2, subln_g, lambda_init):
    B, T, _ = q.shape
    f32 = jnp.float32
    q = rms_norm(q.reshape(B, T, DIFF_HEADS, 2, DIFF_HEAD_QK), q_norm_g, QK_NORM_EPS)
    k = rms_norm(k.reshape(B, T, DIFF_HEADS, 2, DIFF_HEAD_QK), k_norm_g, QK_NORM_EPS)
    q = q.transpose(0, 2, 3, 1, 4)
    k = k.transpose(0, 2, 3, 1, 4)
    v = v.reshape(B, T, DIFF_HEADS, DIFF_HEAD_V).transpose(0, 2, 1, 3)
    lam = (jnp.exp(jnp.sum(lq1.astype(f32) * lk1.astype(f32)))
           - jnp.exp(jnp.sum(lq2.astype(f32) * lk2.astype(f32))) + lambda_init)
    slopes = alibi_slopes(DIFF_HEADS)
    scale = DIFF_HEAD_QK ** -0.5
    outs = []
    for blk in range(T // Q_BLOCK):
        q0, q1 = blk * Q_BLOCK, (blk + 1) * Q_BLOCK
        s = jnp.einsum('bhmqd,bhmkd->bhmqk', q[:, :, :, q0:q1], k[:, :, :, :q1]).astype(f32) * scale
        dist = jnp.arange(q0, q1)[:, None] - jnp.arange(q1)[None, :]
        s = s - slopes[None, :, None, None, None] * dist.astype(f32)
        s = jnp.where(dist >= 0, s, NEG_INF)
        p = jax.nn.softmax(s, axis=-1)
        attn = p[:, :, 0] - lam * p[:, :, 1]
        outs.append(jnp.einsum('bhqk,bhkd->bhqd', attn.astype(v.dtype), v[:, :, :q1]))
    o = jnp.concatenate(outs, axis=2).transpose(0, 2, 1, 3)
    o = rms_norm(o, subln_g, SUBLN_EPS).astype(f32) * (1.0 - lambda_init)
    return o.reshape(B, T, DIFF_WIDTH)

def setup_inputs(seed: int = 0) -> dict:
    key = jax.random.key(seed)
    ks = jax.random.split(key, 21)
    f = jnp.float32
    L = DEPTH

    def nrm(k, shape, s):
        return s * jax.random.normal(k, shape, f)

    ramp = (jnp.arange(RWKV_WIDTH, dtype=f) / (RWKV_WIDTH - 1)) ** 0.9
    return {
        "x": jax.random.normal(ks[0], (BATCH, SEQ, D_MODEL), f),
        "norm_g": 1.0 + nrm(ks[1], (L, D_MODEL), 0.02),
        "w_in": nrm(ks[2], (L, D_MODEL, IN_COLS), D_MODEL ** -0.5),
        "shift_mu": jax.random.uniform(ks[3], (L, SHIFT_COLS), f),
        "w0": -6.0 + 5.0 * ramp[None, :] + nrm(ks[4], (L, RWKV_WIDTH), 0.1),
        "w_decay_up": nrm(ks[5], (L, DECAY_LORA, RWKV_WIDTH), 0.1),
        "a0": nrm(ks[6], (L, RWKV_WIDTH), 0.1),
        "w_iclr_up": nrm(ks[7], (L, ICLR_LORA, RWKV_WIDTH), 0.1),
        "k_k": 0.85 + nrm(ks[8], (L, RWKV_WIDTH), 0.05),
        "k_a": 1.0 + nrm(ks[9], (L, RWKV_WIDTH), 0.05),
        "r_k": nrm(ks[10], (L, RWKV_HEADS, RWKV_HEAD), 0.1),
        "ln_x_w": 1.0 + nrm(ks[11], (L, RWKV_WIDTH), 0.02),
        "ln_x_b": nrm(ks[12], (L, RWKV_WIDTH), 0.02),
        "q_norm_g": 1.0 + nrm(ks[13], (L, DIFF_HEAD_QK), 0.02),
        "k_norm_g": 1.0 + nrm(ks[14], (L, DIFF_HEAD_QK), 0.02),
        "lambda_q1": nrm(ks[15], (L, DIFF_HEAD_QK), 0.1),
        "lambda_k1": nrm(ks[16], (L, DIFF_HEAD_QK), 0.1),
        "lambda_q2": nrm(ks[17], (L, DIFF_HEAD_QK), 0.1),
        "lambda_k2": nrm(ks[18], (L, DIFF_HEAD_QK), 0.1),
        "subln_g": 1.0 + nrm(ks[19], (L, DIFF_HEAD_V), 0.02),
        "w_out": nrm(ks[20], (L, D_MIX, D_MODEL), D_MIX ** -0.5),
    }

def reference(x, norm_g, w_in, shift_mu, w0, w_decay_up, a0, w_iclr_up, k_k, k_a, r_k,
              ln_x_w, ln_x_b, q_norm_g, k_norm_g, lambda_q1, lambda_k1, lambda_q2, lambda_k2,
              subln_g, w_out):
    f32 = jnp.float32
    h = x
    for l in range(DEPTH):
        hn = rms_norm(h, norm_g[l], NORM_EPS)
        proj = jnp.einsum('btd,de->bte', hn, w_in[l])
        shifted = token_shift(proj[..., :SHIFT_COLS], shift_mu[l])
        r, k, v, zw, za = jnp.split(shifted, SHIFT_SPLIT, axis=-1)
        g_a, dq, dk, dv, g_b = jnp.split(proj[..., SHIFT_COLS:], REST_SPLIT, axis=-1)
        lambda_init = 0.8 - 0.6 * math.exp(-0.3 * l)
        y_a = rwkv7_branch(r, k, v, zw, za, w0[l], w_decay_up[l], a0[l], w_iclr_up[l],
                           k_k[l], k_a[l], r_k[l], ln_x_w[l], ln_x_b[l])
        y_b = diff_attention_branch(dq, dk, dv, q_norm_g[l], k_norm_g[l], lambda_q1[l], lambda_k1[l],
                                    lambda_q2[l], lambda_k2[l], subln_g[l], lambda_init)
        mixed = jnp.concatenate([y_a * jax.nn.silu(g_a.astype(f32)),
                                 y_b * jax.nn.silu(g_b.astype(f32))], axis=-1)
        h = h + jnp.einsum('bte,ed->btd', mixed.astype(h.dtype), w_out[l])
    return h


_drawn_inputs = setup_inputs


def setup_inputs(seed=0):
    import zlib

    import numpy as np

    out = dict(_drawn_inputs(seed))
    spreads = {}
    factors = {'a0': 3.469,
     'k_k': 4.098,
     'k_a': 2.67,
     'ln_x_w': 7.509,
     'ln_x_b': 7.805,
     'q_norm_g': 8.0,
     'k_norm_g': 8.0,
     'lambda_q1': 3.262,
     'lambda_k1': 4.463,
     'lambda_q2': 3.48,
     'lambda_k2': 7.0,
     'subln_g': 8.0}
    for name, (base, spread) in spreads.items():
        noise = np.random.default_rng([zlib.crc32(name.encode()), seed]).standard_normal(out[name].shape)
        drawn = base * np.exp(spread * noise) if base else spread * noise
        out[name] = __import__('jax').numpy.asarray(drawn.astype(out[name].dtype))
    for name, factor in factors.items():
        out[name] = (out[name] * factor).astype(out[name].dtype)
    return out
```

```python
from contextlib import ExitStack

import numpy as np
import concourse.bass as bass
from concourse import mybir

F32 = mybir.dt.float32
F32R = mybir.dt.float32r
ALU = mybir.AluOpType
ACT = mybir.ActivationFunctionType
AX_X = mybir.AxisListType.X

P = 128
SEQ = 1024
D_MODEL = 1024
KT = D_MODEL // P
TT = SEQ // P
HALF = 512
GROUPS = 4
HEAD = 64
CH = 64
NCH = SEQ // CH
SUB = 16
BLK = SUB * SUB
JOBS = 8
DECAY_MAX = float(np.exp(-0.5))
NORM_EPS = 1e-6
GN_EPS = 64e-5
SUBLN_EPS = 1e-5
LAMBDA_INIT = 0.8 - 0.6
PAD = 4

MU_R, MU_K, MU_V, W0, A0, K_K, K_A, R_K, LN_W, LN_B = range(10)
N_PRM = 10
OM_R, OM_K, OM_V, OM_KA, HALF_W0, HALF_A0 = range(10, 16)
N_DER = 16
MU_Z, Q_G, K_G, SUB_G, OM_Z, Q_GS, SUB_GS = range(7)
C_ID, C_AV64, C_AV128, C_AMASK, C_M1, C_M2, C_EYE = 0, 128, 256, 384, 512, 576, 640
C_WIDTH = 640 + BLK


def build(nc, ctx, x, w_all, prm, shared, lam_in, norm_g, w_lora, consts, alibi, out,
          mixed_dram, nblk_dram, xblk_dram):

    def sem(name):
        return ctx.enter_context(nc.semaphore(name))

    def sb(name, shape, dt=F32):
        return ctx.enter_context(nc.sbuf_tensor(name, shape, dt))

    proj_ps = ctx.enter_context(nc.psum_tensor("proj_ps", [P, 2, HALF], F32))
    stat_ps = ctx.enter_context(nc.psum_tensor("stat_ps", [P, HALF], F32))
    rk_ps = ctx.enter_context(nc.psum_tensor("rk_ps", [P, 2, HALF], F32))
    at_ps = ctx.enter_context(nc.psum_tensor("at_ps", [P, 3, HALF], F32))

    hn_hi = sb("hn_hi", [P, KT, SEQ], F32R)
    hn_lo = sb("hn_lo", [P, KT, SEQ], F32R)
    w_raw = sb("w_raw", [P, 2, SEQ])
    w_hi = sb("w_hi", [P, 2, SEQ], F32R)
    w_lo = sb("w_lo", [P, 2, SEQ], F32R)
    cst = sb("cst", [P, C_WIDTH])
    ident = cst[:, C_ID:C_ID + P]
    av64 = cst[:, C_AV64:C_AV64 + P]
    av128 = cst[:, C_AV128:C_AV128 + P]
    eps = sb("eps", [P, 4])
    zero_t = sb("zero_t", [P, CH])
    out_banks = [proj_ps[:, 0, :], proj_ps[:, 1, :], rk_ps[:, 0, :], rk_ps[:, 1, :],
                 at_ps[:, 0, :], at_ps[:, 1, :], at_ps[:, 2, :], stat_ps[:]]
    amask = cst[:, C_AMASK:C_AMASK + 2 * CH]
    m1mask = cst[:, C_M1:C_M1 + CH]
    m2mask = cst[:, C_M2:C_M2 + CH]

    loop_mem = ExitStack()

    def lb(name, shape, dt=F32):
        return loop_mem.enter_context(nc.sbuf_tensor(name, shape, dt))

    prm_all = lb("prm_all", [P, GROUPS, N_DER])
    shr = lb("shr", [P, 8])
    ng = lb("ng", [P, KT])
    lam_sb = lb("lam_sb", [P, 4, HEAD])
    small = lb("small", [P, 32])
    cur = lb("cur", [P, N_DER])
    wlora_all = lb("wlora_all", [P, GROUPS, P])
    wlora = lb("wlora", [P, P])
    z_t = lb("z_t", [P, SEQ])
    shift_raw = lb("shift_raw", [P, PAD + SEQ])
    bias_t = lb("bias_t", [P, SEQ])
    k_b = lb("k_b", [P, SEQ])
    r_b = lb("r_b", [P, SEQ])
    v_b = lb("v_b", [P, SEQ])
    kk_b = lb("kk_b", [P, SEQ])
    bonus = lb("bonus", [P, SEQ])
    ar_t = lb("ar_t", [P, NCH, 2, CH])
    work = lb("work", [P, 7, SEQ])
    v_t = lb("v_t", [P, NCH, CH])
    b_t = lb("b_t", [P, NCH, CH])
    k_t = lb("k_t", [P, NCH, CH])
    s_t = lb("s_t", [P, 2, CH])
    sp_t = lb("sp_t", [P, CH])
    u0_t = lb("u0_t", [P, CH])
    u_t = lb("u_t", [P, 2, CH])
    pc = lb("pc", [P, NCH])
    q_b = lb("q_b", [P, SEQ])
    kq_b = lb("kq_b", [P, SEQ])
    val = lb("val", [P, TT, P])
    sc_b = lb("sc_b", [P, 2, SEQ])
    attn_t = lb("attn_t", [P, TT, P])
    o_b = lb("o_b", [P, SEQ])

    lw, cc, aa, e1, ex, sq, nrm = (work[:, i, :] for i in range(7))
    ab_m = work[:, 0:2, :].rearrange("p a (c x t) -> p (a c) x t", x=2, t=CH)
    ak_m = work[:, 2:4, :].rearrange("p a (c x t) -> p (a c) x t", x=2, t=CH)
    x_m = work[:, 4, :].rearrange("p (c t) -> p c t", t=CH)
    xt_m = work[:, 5, :].rearrange("p (c t) -> p c t", t=CH)
    w_m = work[:, 6, :].rearrange("p (c t) -> p c t", t=CH)
    nblk = work[:, 6, 0:BLK].rearrange("p (s t) -> p s t", t=SUB)
    xblk = work[:, 6, BLK:2 * BLK].rearrange("p (t s) -> p t s", s=SUB)
    xblkt = work[:, 6, 2 * BLK:3 * BLK].rearrange("p (s t) -> p s t", t=SUB)
    prod = work[:, 6, 3 * BLK:4 * BLK].rearrange("p (t s) -> p t s", s=SUB)
    x_in = [k_b, r_b, v_b, kk_b, bonus, q_b, kq_b, o_b]
    y_b, ga_b, gb_b = k_b, r_b, kk_b
    mx, nm, ls, rl, c1 = small[:, 0:4], small[:, 4:6], small[:, 6:8], small[:, 8:10], small[:, 10:11]
    lam_neg = small[:, 11:12]
    ssq, rstd = small[:, 12:20], small[:, 20:28]
    lam_dot, lam_e = small[:, 28:30], small[:, 30:32]
    x_scr = [work[:, 0, :], work[:, 1, :]]
    y_sqs, y_nrm = v_b[:, 0:HALF], v_b[:, HALF:SEQ]
    o_sqs, o_nrm = work[:, 6, 0:HALF], work[:, 6, HALF:SEQ]
    ga_th, gb_th = o_b, shift_raw[:, PAD:PAD + SEQ]
    qk_sqs = o_b
    qk_nrm = val.rearrange("p a b -> p (a b)")


    loop_mem.close()
    wo_hi = sb("wo_hi", [P, KT, SEQ], F32R)
    wo_lo = sb("wo_lo", [P, KT, SEQ], F32R)
    m_raw = sb("m_raw", [P, 2, SEQ])
    x_res = sb("x_res", [P, 2, SEQ])
    o_stage = sb("o_stage", [P, 2, SEQ])

    c_loaded = sem("c_loaded")
    x_loaded = [sem(f"x_loaded{t}") for t in range(TT)]
    w_loaded = [sem("w_loaded0"), sem("w_loaded1")]
    w_hi_done, w_split = sem("w_hi_done"), sem("w_split")
    proj_full, proj_free = sem("proj_full"), sem("proj_free")
    ssq_done, xn_done = sem("ssq_done"), sem("xn_done")
    turned, hi_done, hn_done = sem("turned"), sem("hi_done"), sem("hn_done")
    prm_done, lam_exp, z_shifted, z_done = sem("prm_done"), sem("lam_exp"), sem("z_shifted"), sem("z_done")
    group_set = sem("group_set")
    shifted = sem("shifted")
    stat_full, stat_free = sem("stat_full"), sem("stat_free")
    kk_squared, rk_in = sem("kk_squared"), sem("rk_in")
    scanned, exps_done = sem("scanned"), sem("exps_done")
    tildes = sem("tildes")
    qk_done = sem("qk_done")
    rk_full, rk_free = sem("rk_full"), sem("rk_free")
    nblk_out, nblk_in = sem("nblk_out"), sem("nblk_in")
    blocks_done, xblk_out, xblk_in = sem("blocks_done"), sem("xblk_out"), sem("xblk_in")
    x_zeroed = sem("x_zeroed")
    step_full = sem("step_full")
    u0_done, u_done, s_done = sem("u0_done"), sem("u_done"), sem("s_done")
    y_full, y_out = sem("y_full"), sem("y_out")
    y_sq, y_fin = sem("y_sq"), sem("y_fin")
    at_full, at_free = sem("at_full"), sem("at_free")
    neg_done, exp_done, attn_done = sem("neg_done"), sem("exp_done"), sem("attn_done")
    o_sq, o_fin = sem("o_sq"), sem("o_fin")
    bias_in, mixed_out = sem("bias_in"), sem("mixed_out")
    m_in = [sem("m_in0"), sem("m_in1")]
    m_hi_done, m_split = sem("m_hi_done"), sem("m_split")
    wo_hi_done, wo_split = sem("wo_hi_done"), sem("wo_split")
    res_in = [sem("res_in0"), sem("res_in1")]
    out_full, out_sum = sem("out_full"), sem("out_sum")
    stored = [sem("stored0"), sem("stored1")]

    STATS = ["dec0", "dec1", "icl0", "icl1", "kk0", "kk1", "rk0", "rk1", "q0", "q1", "k0", "k1",
             "ym0", "yv0", "om0", "ym1", "yv1", "om1"]
    NST = len(STATS)
    stat_no = {s: n for n, s in enumerate(STATS)}
    RK_JOBS = ([("turn", a, h) for h in range(2) for a in range(3)]
               + [("ab", q) for q in range(4)] + [("ak", q) for q in range(4)]
               + [("merge", m, h) for m in range(5) for h in range(2)])
    NRK = len(RK_JOBS)
    rk_no = {j: n for n, j in enumerate(RK_JOBS)}
    AT_JOBS = [("v", 0), ("v", 1)]
    for qb in range(TT):
        nh = qb // 4 + 1
        AT_JOBS += [("s", qb, m, c) for m in range(2) for c in range(nh)]
        AT_JOBS += [("t", qb, c) for c in range(nh)] + [("o", qb)]
    NAT = len(AT_JOBS)
    at_no = {j: n for n, j in enumerate(AT_JOBS)}
    NPJ = 2 * JOBS
    NSTEP = 3 * NCH

    def cols(h):
        return slice(h * HALF, (h + 1) * HALF)

    def rows(h):
        return slice(h * HEAD, (h + 1) * HEAD)

    passed = {e.engine: sem(f"passed{i}") for i, e in enumerate((nc.tensor, nc.vector, nc.gpsimd, nc.sync))}

    def settled(eng):
        eng.sem_inc(passed[eng.engine], 1)

    block = ctx.enter_context(nc.Block())

    @block.sync
    def _(sp):
        for t in range(TT):
            sp.dma_start(x_in[t][:], x[t * P:(t + 1) * P, :]).then_inc(x_loaded[t], 16)
        sp.dma_start(cst[:], consts).then_inc(c_loaded, 16)
        sp.dma_start(prm_all[:, :, 0:N_PRM], prm).then_inc(c_loaded, 16)
        sp.dma_start(shr[:, 0:4], shared).then_inc(c_loaded, 16)
        sp.dma_start(ng[:], norm_g).then_inc(c_loaded, 16)
        sp.dma_start(lam_sb[:], lam_in).then_inc(c_loaded, 16)
        sp.dma_start(wlora_all[:], w_lora).then_inc(c_loaded, 16)
        for j in range(2):
            sp.dma_start(w_raw[:, j, :], w_all[j]).then_inc(w_loaded[j], 16)
        sp.wait_ge(w_split, 1)
        sp.dma_start(w_raw[:, 0, :], w_all[2]).then_inc(w_loaded[0], 16)
        with sp.Fori(0, GROUPS) as g:
            sp.wait_ge(at_free, g * NAT)
            settled(sp)
            sp.dma_start(bias_t[:], alibi[bass.ds(g, 1)].rearrange("o p c -> (o p) c")).then_inc(bias_in, 16)
            for j in range(JOBS):
                sp.wait_ge(w_split, g * JOBS + (j + 2))
                sp.dma_start(w_raw[:, (j + 1) % 2, :],
                             w_all[bass.ds(g * JOBS + (j + 3), 1)].rearrange("o p c -> (o p) c")
                             ).then_inc(w_loaded[(j + 1) % 2], 16)
                if j == 4:
                    sp.wait_ge(rk_free, g * NRK + (rk_no["ab", 3] + 1))
                    for i in range(8):
                        sp.dma_start(nblk_dram[i].rearrange("c s t -> s c t"),
                                     ab_m[SUB * i:SUB * i + SUB, :, 0, SUB * (i % 4):SUB * (i % 4) + SUB]
                                     ).then_inc(nblk_out, 16)
                    sp.wait_ge(nblk_out, g * 128 + 128)
                    settled(sp)
                    sp.wait_ge(tildes, g + 1)
                    sp.dma_start(nblk, nblk_dram.rearrange("i c s t -> (i c) s t")).then_inc(nblk_in, 16)
                if j == 5:
                    sp.wait_ge(blocks_done, g + 1)
                    sp.dma_start(xblk_dram[0].rearrange("i c t s -> (i c) t s"), xblk).then_inc(xblk_out, 16)
                    sp.dma_start(xblk_dram[1].rearrange("i c t s -> (i c) t s"), xblkt).then_inc(xblk_out, 16)
                    sp.wait_ge(xblk_out, g * 32 + 32)
                    sp.wait_ge(x_zeroed, g + 1)
                    for n, dst in ((0, x_m), (1, xt_m)):
                        for i in range(8):
                            sp.dma_start(dst[SUB * i:SUB * i + SUB, :, SUB * (i % 4):SUB * (i % 4) + SUB],
                                         xblk_dram[n, i].rearrange("c t s -> t c s")).then_inc(xblk_in, 16)
            sp.wait_ge(o_fin, g * 2 + 2)
            sp.dma_start(mixed_dram[bass.ds(g + GROUPS, 1)].rearrange("o p c -> (o p) c"), o_b[:]).then_inc(mixed_out, 16)
            sp.wait_ge(y_fin, g * 2 + 2)
            sp.dma_start(mixed_dram[bass.ds(g, 1)].rearrange("o p c -> (o p) c"), bonus[:]).then_inc(mixed_out, 16)
        sp.wait_ge(mixed_out, 32 * GROUPS)
        for e in range(KT):
            if e >= 2:
                sp.wait_ge(m_split, e - 1)
            sp.dma_start(m_raw[:, e % 2, :], mixed_dram[e]).then_inc(m_in[e % 2], 16)
            if e >= 2:
                sp.wait_ge(wo_split, e - 1)
                sp.dma_start(w_raw[:, (e + 1) % 2, :], w_all[GROUPS * JOBS + 1 + e]).then_inc(w_loaded[(e + 1) % 2], 16)
        for t in range(TT):
            if t >= 2:
                sp.wait_ge(out_sum, 2 * t - 2)
            sp.dma_start(x_res[:, t % 2, :], x[t * P:(t + 1) * P, :]).then_inc(res_in[t % 2], 16)
            if t >= 1:
                sp.wait_ge(out_sum, 2 * t)
                sp.dma_start(out[(t - 1) * P:t * P, :], o_stage[:, (t - 1) % 2, :]).then_inc(stored[(t - 1) % 2], 16)
        sp.wait_ge(out_sum, 2 * TT)
        sp.dma_start(out[(TT - 1) * P:TT * P, :], o_stage[:, (TT - 1) % 2, :]).then_inc(stored[(TT - 1) % 2], 16)
        for s in stored:
            sp.wait_ge(s, 16 * TT // 2)

    @block.gpsimd
    def _(pool):
        for n in range(2):
            pool.wait_ge(w_hi_done, n + 1)
            nc.gpsimd.tensor_tensor(w_lo[:, n, :], w_raw[:, n, :], w_hi[:, n, :].bitcast(F32),
                                    ALU.subtract).then_inc(w_split, 1)
        with pool.Fori(0, GROUPS) as g:
            for j in range(JOBS):
                if j == 5:
                    pool.wait_ge(stat_free, g * NST + (stat_no["rk1"] + 1))
                    settled(pool)
                    nc.gpsimd.memset(work[:, 4:6, :], 0.0).then_inc(x_zeroed, 1)
                pool.wait_ge(w_hi_done, g * JOBS + (j + 3))
                nc.gpsimd.tensor_tensor(w_lo[:, j % 2, :], w_raw[:, j % 2, :], w_hi[:, j % 2, :].bitcast(F32),
                                        ALU.subtract).then_inc(w_split, 1)
        for e in range(KT):
            pool.wait_ge(wo_hi_done, e + 1)
            nc.gpsimd.tensor_tensor(wo_lo[:, e, :], w_raw[:, (e + 1) % 2, :], wo_hi[:, e, :].bitcast(F32),
                                    ALU.subtract).then_inc(wo_split, 1)

    @block.scalar
    def _(act):
        for t in range(TT):
            act.wait_ge(x_loaded[t], 16)
            if t >= 2:
                act.drain()
            nc.scalar.activation(x_scr[t % 2], x_in[t][:], ACT.Square, accum_out=ssq[:, t:t + 1])
        act.drain()
        act.wait_ge(prm_done, 1)
        nc.scalar.activation(rstd, ssq, ACT.Sqrt, scale=1.0 / D_MODEL, bias=eps[:, 0:1]).then_inc(ssq_done, 1)
        nc.scalar.activation(lam_e, lam_dot, ACT.Exp).then_inc(lam_exp, 1)
        for n in range(2):
            act.wait_ge(w_loaded[n], 16)
            nc.scalar.activation(w_hi[:, n, :], w_raw[:, n, :], ACT.Copy).then_inc(w_hi_done, 1)
        for n in range(2 * KT):
            act.wait_ge(turned, n + 1)
            nc.scalar.activation(hn_hi[:, n // 2, cols(n % 2)], at_ps[:, n % 3, :], ACT.Copy,
                                 scale=ng[:, n // 2:n // 2 + 1]).then_inc(hi_done, 1)
        for h in range(2):
            act.wait_ge(proj_full, h + 1)
            nc.scalar.activation(shift_raw[:, PAD + h * HALF:PAD + (h + 1) * HALF], proj_ps[:, h, :], ACT.Copy)
            nc.scalar.activation(z_t[:, cols(h)], proj_ps[:, h, :], ACT.Copy,
                                 scale=shr[:, OM_Z:OM_Z + 1]).then_inc(proj_free, 1)
        act.wait_ge(z_shifted, 1)
        nc.scalar.activation(z_t[0:HEAD, :], z_t[0:HEAD, :], ACT.Tanh).then_inc(z_done, 1)

        with act.Fori(0, GROUPS) as g:
            def next_hi(j):
                act.wait_ge(w_loaded[j % 2], g * 64 + 16 * (j // 2 + 2))
                act.wait_ge(proj_full, g * NPJ + (2 + 2 * j))
                nc.scalar.activation(w_hi[:, j % 2, :], w_raw[:, j % 2, :], ACT.Copy).then_inc(w_hi_done, 1)

            def take_shifted(j, h, dst, om):
                act.wait_ge(proj_full, g * NPJ + (3 + 2 * j + h))
                nc.scalar.activation(shift_raw[:, PAD + h * HALF:PAD + (h + 1) * HALF], proj_ps[:, h, :], ACT.Copy)
                nc.scalar.activation(dst[:, cols(h)], proj_ps[:, h, :], ACT.Copy,
                                     scale=cur[:, om:om + 1]).then_inc(proj_free, 1)

            def take_two(j, h, dst, dst2, func, scale):
                act.wait_ge(proj_full, g * NPJ + (3 + 2 * j + h))
                nc.scalar.activation(dst[:, cols(h)], proj_ps[:, h, :], ACT.Copy)
                nc.scalar.activation(dst2[:, cols(h)], proj_ps[:, h, :], func, scale=scale).then_inc(proj_free, 1)

            def stat_to(name, dst, func, scale=1.0, bias=0.0):
                act.wait_ge(stat_full, g * NST + (stat_no[name] + 1))
                nc.scalar.activation(dst, stat_ps[:], func, scale=scale, bias=bias).then_inc(stat_free, 1)

            half_w0, half_a0 = cur[:, HALF_W0:HALF_W0 + 1], cur[:, HALF_A0:HALF_A0 + 1]
            next_hi(0)
            act.wait_ge(group_set, g + 1)
            act.wait_ge(o_fin, g * 2)
            act.wait_ge(y_fin, g * 2)
            stat_to("dec0", lw[:, 0:HALF], ACT.Tanh, 0.5, half_w0)
            take_shifted(0, 0, k_b, OM_K)
            stat_to("dec1", lw[:, HALF:SEQ], ACT.Tanh, 0.5, half_w0)
            take_shifted(0, 1, k_b, OM_K)
            next_hi(1)
            act.wait_ge(shifted, g * 3 + 1)
            nc.scalar.activation(sq, k_b[:], ACT.Square, scale=cur[:, K_K:K_K + 1]).then_inc(kk_squared, 1)
            stat_to("icl0", aa[:, 0:HALF], ACT.Tanh, 0.5, half_a0)
            take_shifted(1, 0, r_b, OM_R)
            stat_to("icl1", aa[:, HALF:SEQ], ACT.Tanh, 0.5, half_a0)
            take_shifted(1, 1, r_b, OM_R)
            next_hi(2)
            act.wait_ge(scanned, g + 1)
            nc.scalar.activation(e1, cc, ACT.Exp)
            nc.scalar.activation(ex, ex, ACT.Exp)
            act.drain()
            nc.scalar.activation(cc, cc, ACT.Exp, scale=-1.0).then_inc(exps_done, 1)
            act.wait_ge(shifted, g * 3 + 2)
            stat_to("kk0", nrm[:, 0:HALF], ACT.Sqrt, float(HEAD))
            take_shifted(2, 0, v_b, OM_V)
            stat_to("kk1", nrm[:, HALF:SEQ], ACT.Sqrt, float(HEAD))
            take_shifted(2, 1, v_b, OM_V)
            next_hi(3)
            act.wait_ge(mixed_out, g * 32)
            for h in range(2):
                take_two(3, h, q_b, qk_sqs, ACT.Square, 1.0)
            next_hi(4)
            for h in range(2):
                stat_to(f"q{h}", qk_nrm[:, cols(h)], ACT.Sqrt, 1.0, eps[:, 0:1])
                take_two(4, h, kq_b, qk_sqs, ACT.Square, 1.0)
            next_hi(5)
            act.wait_ge(qk_done, g * 2 + 1)
            for h in range(2):
                stat_to(f"k{h}", qk_nrm[:, cols(h)], ACT.Sqrt, 1.0, eps[:, 0:1])
            act.wait_ge(rk_free, g * NRK + (rk_no["turn", 0, 1] + 1))
            for h in range(2):
                act.wait_ge(proj_full, g * NPJ + (3 + 2 * 5 + h))
                nc.scalar.activation(v_b[:, cols(h)], proj_ps[:, h, :], ACT.Copy).then_inc(proj_free, 1)
            next_hi(6)
            for h in range(2):
                take_two(6, h, r_b, ga_th, ACT.Tanh, 0.5)
            next_hi(7)

            def y_square(h):
                act.wait_ge(stat_free, g * NST + (stat_no[f"ym{h}"] + 1))
                act.wait_ge(y_fin, g * 2 + h)
                nc.scalar.activation(y_sqs, y_b[:, cols(h)], ACT.Square).then_inc(y_sq, 1)

            def o_square(h):
                act.wait_ge(at_free, g * NAT + (at_no["o", 4 * h + 3] + 1))
                act.wait_ge(o_fin, g * 2 + h)
                nc.scalar.activation(o_sqs, o_b[:, cols(h)], ACT.Square).then_inc(o_sq, 1)

            for c in range(0, NCH, 2):
                qb = c // 2
                act.wait_ge(neg_done, g * TT + (qb + 1))
                for m in range(2):
                    ins = nc.scalar.activation(sc_b[:, m, 0:P * (qb + 1)], sc_b[:, m, 0:P * (qb + 1)], ACT.Exp,
                                               bias=nm[:, m:m + 1], accum_out=ls[:, m:m + 1])
                ins.then_inc(exp_done, 1)
                if c == 8:
                    take_two(7, 0, gb_b, gb_th, ACT.Tanh, 0.5)
                    o_square(0)
                    y_square(0)
                if c == 10:
                    stat_to("yv0", y_nrm, ACT.Sqrt, 1.0, eps[:, 1:2])
                    stat_to("om0", o_nrm, ACT.Sqrt, 1.0, eps[:, 2:3])
            take_two(7, 1, gb_b, gb_th, ACT.Tanh, 0.5)
            y_square(1)
            o_square(1)
            stat_to("yv1", y_nrm, ACT.Sqrt, 1.0, eps[:, 1:2])
            stat_to("om1", o_nrm, ACT.Sqrt, 1.0, eps[:, 2:3])

        act.wait_ge(mixed_out, 32 * GROUPS)
        act.wait_ge(proj_full, GROUPS * NPJ + 2)
        for e in range(KT):
            act.wait_ge(m_in[e % 2], 16 * (e // 2 + 1))
            nc.scalar.activation(hn_hi[:, e, :], m_raw[:, e % 2, :], ACT.Copy).then_inc(m_hi_done, 1)
            s = (e + 1) % 2
            act.wait_ge(w_loaded[s], 16 * ((GROUPS * JOBS + 1 + e) // 2 + 1))
            nc.scalar.activation(wo_hi[:, e, :], w_raw[:, s, :], ACT.Copy).then_inc(wo_hi_done, 1)

    @block.vector
    def _(dve):
        V = nc.vector

        def affine(dst, src, a, b):
            return V.tensor_scalar(dst, src, a, b, ALU.mult, ALU.add)

        V.memset(shift_raw[:, 0:PAD], 0.0)
        V.memset(zero_t[:], 0.0)
        V.memset(eps[:, 0:1], NORM_EPS)
        V.memset(eps[:, 1:2], GN_EPS)
        V.memset(eps[:, 2:3], SUBLN_EPS)
        dve.wait_ge(c_loaded, 16 * 6)
        affine(prm_all[:, :, OM_R:OM_V + 1], prm_all[:, :, MU_R:MU_V + 1], -1.0, 1.0)
        affine(prm_all[:, :, OM_KA:OM_KA + 1], prm_all[:, :, K_A:K_A + 1], -1.0, 1.0)
        V.tensor_scalar(prm_all[:, :, HALF_W0:HALF_A0 + 1], prm_all[:, :, W0:A0 + 1], 0.5, None, ALU.mult)
        affine(shr[:, OM_Z:OM_Z + 1], shr[:, MU_Z:MU_Z + 1], -1.0, 1.0)
        V.tensor_scalar(shr[:, Q_GS:Q_GS + 1], shr[:, Q_G:Q_G + 1], HEAD ** -0.5, None, ALU.mult)
        V.tensor_scalar(shr[:, SUB_GS:SUB_GS + 1], shr[:, SUB_G:SUB_G + 1], 1.0 - LAMBDA_INIT, None, ALU.mult)
        V.tensor_tensor(lam_sb[:, 0:2, :], lam_sb[:, 0:2, :], lam_sb[:, 2:4, :], ALU.mult)
        dve.drain()
        V.tensor_reduce(lam_dot, lam_sb[:, 0:2, :], AX_X, ALU.add).then_inc(prm_done, 1)
        dve.wait_ge(ssq_done, 1)
        V.reciprocal(rstd, rstd)
        dve.drain()
        for t in range(TT):
            V.tensor_scalar(x_in[t][:], x_in[t][:], rstd[:, t:t + 1], None, ALU.mult).then_inc(xn_done, 1)
        dve.wait_ge(lam_exp, 1)
        V.tensor_scalar(lam_neg, lam_e[:, 1:2], lam_e[:, 0:1], -LAMBDA_INIT, ALU.subtract, ALU.add)
        for n in range(2 * KT):
            dve.wait_ge(hi_done, n + 1)
            V.scalar_tensor_tensor(out=hn_lo[:, n // 2, cols(n % 2)], in0=at_ps[:, n % 3, :],
                                   scalar=ng[:, n // 2:n // 2 + 1], in1=hn_hi[:, n // 2, cols(n % 2)].bitcast(F32),
                                   op0=ALU.mult, op1=ALU.subtract).then_inc(hn_done, 1)
        dve.wait_ge(proj_free, 2)
        V.scalar_tensor_tensor(out=z_t[:], in0=shift_raw[:, PAD - 1:PAD - 1 + SEQ], scalar=shr[:, MU_Z:MU_Z + 1],
                               in1=z_t[:], op0=ALU.mult, op1=ALU.add).then_inc(z_shifted, 1)

        with dve.Fori(0, GROUPS) as g:
            def prm1(i):
                return cur[:, i:i + 1]

            def stt(dst, a, s, b, op0=ALU.mult, op1=ALU.mult):
                return V.scalar_tensor_tensor(out=dst, in0=a, scalar=s, in1=b, op0=op0, op1=op1)

            def mul(dst, a, b):
                return V.tensor_tensor(dst, a, b, ALU.mult)

            def shift(j, dst, mu):
                dve.wait_ge(proj_free, g * NPJ + (4 + 2 * j))
                stt(dst[:], shift_raw[:, PAD - 1:PAD - 1 + SEQ], prm1(mu), dst[:], ALU.mult, ALU.add).then_inc(shifted, 1)

            def rk_take(job):
                n = rk_no[job]
                dve.wait_ge(rk_full, g * NRK + (n + 1))
                return rk_ps[:, n % 2, :]

            def at_take(job):
                n = at_no[job]
                dve.wait_ge(at_full, g * NAT + (n + 1))
                return at_ps[:, n % 3, :]

            def sigmoid(buf):
                return affine(buf, buf, 0.5, 0.5)

            V.tensor_copy(cur[:], prm_all[:, bass.ds(g, 1), :].rearrange("p o n -> p (o n)"))
            V.tensor_copy(wlora[:], wlora_all[:, bass.ds(g, 1), :].rearrange("p o n -> p (o n)"))
            dve.drain().then_inc(group_set, 1)
            shift(0, k_b, MU_K)
            dve.wait_ge(stat_free, g * NST + 2)
            affine(lw, lw, -0.5 * DECAY_MAX, -0.5 * DECAY_MAX)
            dve.drain()
            for c in range(NCH):
                s = slice(c * CH, (c + 1) * CH)
                V.tensor_tensor_scan(cc[:, s], lw[:, s], zero_t[:], 0.0, ALU.add, ALU.add)
            dve.drain()
            V.tensor_tensor(ex, cc, lw, ALU.subtract).then_inc(scanned, 1)
            dve.wait_ge(stat_free, g * NST + 4)
            sigmoid(aa)
            shift(1, r_b, MU_R)
            dve.drain()
            V.tensor_scalar(lw, aa, prm1(K_A), prm1(OM_KA), ALU.mult, ALU.add)
            dve.wait_ge(stat_free, g * NST + 6)
            V.tensor_scalar(nrm, nrm, 1e-12, None, ALU.max)
            dve.drain()
            V.reciprocal(nrm, nrm)
            dve.drain()
            stt(kk_b[:], k_b[:], prm1(K_K), nrm)
            dve.drain()
            mul(k_b[:], k_b[:], lw)
            shift(2, v_b, MU_V)
            dve.drain()
            stt(sq, r_b[:], prm1(R_K), k_b[:]).then_inc(rk_in, 1)
            dve.wait_ge(exps_done, g + 1)
            V.tensor_copy(pc[:], e1.rearrange("p (c t) -> p c t", t=CH)[:, :, CH - 1])
            ch3 = lambda ap: ap.rearrange("p (c t) -> p c t", t=CH)
            mul(ar_t[:, :, 1, :], ch3(r_b[:]), ch3(e1))
            stt(ar_t[:, :, 0, :], ch3(kk_b[:]), -1.0, ch3(ex))
            dve.drain()
            mul(kk_b[:], kk_b[:], aa)
            mul(k_b[:], k_b[:], cc)
            dve.drain()
            mul(kk_b[:], kk_b[:], cc).then_inc(tildes, 1)
            dve.wait_ge(mixed_out, g * 32)
            for h in range(2):
                dve.wait_ge(stat_full, g * NST + (stat_no[f"rk{h}"] + 1))
                stt(bonus[:, cols(h)], stat_ps[:], float(HEAD), v_b[:, cols(h)]).then_inc(stat_free, 1)
            dve.wait_ge(stat_free, g * NST + (stat_no["q1"] + 1))
            V.reciprocal(qk_nrm, qk_nrm)
            dve.drain()
            stt(q_b[:], q_b[:], shr[:, Q_GS:Q_GS + 1], qk_nrm).then_inc(qk_done, 1)
            for h in range(2):
                for a, dst in enumerate((v_t, b_t, k_t)):
                    V.tensor_copy(dst[:, 8 * h:8 * h + 8, :], rk_take(("turn", a, h)).rearrange("p (c d) -> p c d", d=CH)
                                  ).then_inc(rk_free, 1)
            for name, dst in (("ab", ab_m), ("ak", ak_m)):
                for q in range(4):
                    V.tensor_tensor(dst[:, 4 * q:4 * q + 4, :, :].rearrange("p c x t -> p c (x t)"),
                                    rk_take((name, q)).rearrange("p (c t) -> p c t", c=4),
                                    amask.unsqueeze(1).broadcast_to([P, 4, 2 * CH]), ALU.mult).then_inc(rk_free, 1)
            dve.wait_ge(stat_free, g * NST + (stat_no["k1"] + 1))
            V.reciprocal(qk_nrm, qk_nrm)
            dve.drain()
            stt(kq_b[:], kq_b[:], shr[:, K_G:K_G + 1], qk_nrm).then_inc(qk_done, 1)
            V.tensor_copy(xblk.rearrange("p t s -> p (t s)"), cst[:, C_EYE:C_EYE + BLK])
            dve.wait_ge(nblk_in, g * 16 + 16)
            settled(dve)
            for t in range(1, SUB):
                dve.drain()
                mul(prod[:, 0:t, 0:t], xblk[:, 0:t, 0:t].rearrange("p s j -> p j s"),
                    nblk[:, 0:t, t].unsqueeze(1).broadcast_to([P, t, t]))
                dve.drain()
                V.tensor_reduce(xblk[:, t, 0:t], prod[:, 0:t, 0:t], AX_X, ALU.add)
            dve.drain()
            V.tensor_copy(xblkt, xblk.rearrange("p t s -> p s t")).then_inc(blocks_done, 1)
            for n in range(2):
                V.tensor_copy(val[:, 4 * n:4 * n + 4, :], at_take(("v", n)).rearrange("p (a d) -> p a d", d=P)
                              ).then_inc(at_free, 1)
            dve.wait_ge(proj_free, g * NPJ + (4 + 2 * 6))
            sigmoid(ga_th[:])
            dve.drain()
            mul(ga_b[:], ga_b[:], ga_th[:])
            def merged(m, h):
                return rk_take(("merge", m, h)).rearrange("p (c d) -> p c d", d=CH)

            for m, dst, mask in ((0, w_m, m1mask), (1, x_m, None), (2, xt_m, None), (3, w_m, m2mask), (4, xt_m, None)):
                for h in range(2):
                    part = dst[:, 8 * h:8 * h + 8, :]
                    if mask is not None:
                        V.tensor_tensor(part, merged(m, h), mask.unsqueeze(1).broadcast_to([P, 8, CH]),
                                        ALU.mult).then_inc(rk_free, 1)
                    else:
                        V.tensor_tensor(part, merged(m, h), part, ALU.add).then_inc(rk_free, 1)
            V.memset(s_t[:, 0, :], 0.0).then_inc(s_done, 1)

            def scores(qb, m):
                nh = qb // 4 + 1
                if qb == 0 and m == 0:
                    dve.wait_ge(bias_in, g * 16 + 16)
                for c in range(nh):
                    w = min(HALF, P * (qb + 1) - HALF * c)
                    off = SEQ - P - P * qb + HALF * c
                    bank = at_take(("s", qb, m, c))
                    settled(dve)
                    V.tensor_tensor_reduce(out=sc_b[:, m, HALF * c:HALF * c + w],
                                           in0=bank[:, 0:w], in1=bias_t[:, off:off + w],
                                           scale=1.0, scalar=-3e38, op0=ALU.add, op1=ALU.max,
                                           accum_out=mx[:, 2 * m + c:2 * m + c + 1]).then_inc(at_free, 1)

            def negate(qb):
                dve.drain()
                for m in range(2):
                    if qb < 4:
                        ins = V.tensor_scalar(nm[:, m:m + 1], mx[:, 2 * m:2 * m + 1], -1.0, None, ALU.mult)
                    else:
                        ins = V.tensor_scalar(nm[:, m:m + 1], mx[:, 2 * m:2 * m + 1], mx[:, 2 * m + 1:2 * m + 2],
                                              -1.0, ALU.max, ALU.mult)
                ins.then_inc(neg_done, 1)

            def weigh(qb):
                dve.wait_ge(exp_done, g * TT + (qb + 1))
                V.reciprocal(rl, ls)
                dve.drain()
                mul(c1, rl[:, 1:2], lam_neg)
                dve.drain()
                n = P * (qb + 1)
                V.tensor_scalar(sc_b[:, 1, 0:n], sc_b[:, 1, 0:n], c1, None, ALU.mult)

            def combine(qb):
                n = P * (qb + 1)
                dve.drain()
                stt(sc_b[:, 0, 0:n], sc_b[:, 0, 0:n], rl[:, 0:1], sc_b[:, 1, 0:n], ALU.mult, ALU.add).then_inc(attn_done, 1)

            def turned_attn(qb):
                for c in range(qb // 4 + 1):
                    w = min(4, qb + 1 - 4 * c)
                    V.tensor_copy(attn_t[:, 4 * c:4 * c + w, :],
                                  at_take(("t", qb, c))[:, 0:w * P].rearrange("p (a d) -> p a d", d=P)).then_inc(at_free, 1)

            def attn_out(qb):
                V.tensor_copy(o_b[:, P * qb:P * qb + P], at_take(("o", qb))[:, 0:P]).then_inc(at_free, 1)

            def y_take(h):
                dve.wait_ge(y_full, g * 2 + h + 1)
                V.tensor_copy(y_b[:, cols(h)], rk_ps[:, 1, :]).then_inc(y_out, 1)

            def y_centre(h):
                dve.wait_ge(stat_full, g * NST + (stat_no[f"ym{h}"] + 1))
                V.tensor_tensor(y_b[:, cols(h)], y_b[:, cols(h)], stat_ps[:], ALU.subtract).then_inc(stat_free, 1)

            def y_finish(h):
                dve.wait_ge(stat_free, g * NST + (stat_no[f"yv{h}"] + 1))
                V.reciprocal(y_nrm, y_nrm)
                dve.drain()
                mul(y_b[:, cols(h)], y_b[:, cols(h)], y_nrm)
                dve.drain()
                affine(y_b[:, cols(h)], y_b[:, cols(h)], prm1(LN_W), prm1(LN_B))
                dve.drain()
                V.tensor_tensor(bonus[:, cols(h)], bonus[:, cols(h)], y_b[:, cols(h)], ALU.add)
                dve.drain()
                mul(bonus[:, cols(h)], bonus[:, cols(h)], ga_b[:, cols(h)]).then_inc(y_fin, 1)

            def gate_b(h):
                dve.wait_ge(proj_free, g * NPJ + (3 + 2 * 7 + h))
                sigmoid(gb_th[:, cols(h)])
                dve.drain()
                mul(gb_b[:, cols(h)], gb_b[:, cols(h)], gb_th[:, cols(h)])

            def o_finish(h):
                dve.wait_ge(stat_free, g * NST + (stat_no[f"om{h}"] + 1))
                V.reciprocal(o_nrm, o_nrm)
                dve.drain()
                stt(o_b[:, cols(h)], o_b[:, cols(h)], shr[:, SUB_GS:SUB_GS + 1], o_nrm)
                dve.drain()
                mul(o_b[:, cols(h)], o_b[:, cols(h)], gb_b[:, cols(h)]).then_inc(o_fin, 1)

            for c in range(NCH):
                qb, odd = c // 2, c % 2
                dve.wait_ge(step_full, g * NSTEP + (3 * c + 1))
                V.tensor_copy(u0_t[:], rk_ps[:, 0, 0:CH]).then_inc(u0_done, 1)
                dve.drain()
                V.tensor_scalar(sp_t[:], s_t[:, c % 2, :], pc[:, c:c + 1], None, ALU.mult)
                if c == 8:
                    y_take(0)
                if not odd:
                    if qb >= 1:
                        attn_out(qb - 1)
                    scores(qb, 0)
                else:
                    weigh(qb)
                dve.wait_ge(step_full, g * NSTEP + (3 * c + 2))
                V.tensor_copy(u_t[:, c % 2, :], rk_ps[:, 0, CH:2 * CH]).then_inc(u_done, 1)
                if not odd:
                    scores(qb, 1)
                    negate(qb)
                else:
                    combine(qb)
                dve.wait_ge(step_full, g * NSTEP + (3 * c + 3))
                stt(s_t[:, (c + 1) % 2, :], rk_ps[:, 0, 2 * CH:3 * CH], pc[:, c:c + 1], sp_t[:], ALU.mult, ALU.add).then_inc(s_done, 1)
                if odd:
                    turned_attn(qb)
                if c == 8:
                    y_centre(0)
                    gate_b(0)
                if c == 13:
                    y_finish(0)
                if c == 14:
                    o_finish(0)
            attn_out(TT - 1)
            y_take(1)
            y_centre(1)
            gate_b(1)
            y_finish(1)
            o_finish(1)

        for e in range(KT):
            dve.wait_ge(m_hi_done, e + 1)
            V.tensor_tensor(hn_lo[:, e, :], m_raw[:, e % 2, :], hn_hi[:, e, :].bitcast(F32), ALU.subtract).then_inc(m_split, 1)
        for t in range(TT):
            dve.wait_ge(res_in[t % 2], 16 * (t // 2 + 1))
            if t >= 2:
                dve.wait_ge(stored[t % 2], 16 * (t // 2))
            for h in range(2):
                n = 2 * t + h
                dve.wait_ge(out_full, n + 1)
                V.tensor_tensor(o_stage[:, t % 2, cols(h)], out_banks[n % 8], x_res[:, t % 2, cols(h)], ALU.add).then_inc(out_sum, 1)

    @block.tensor
    def _(pe):
        T = nc.tensor

        def three(bank, w_h, w_l, x_h, x_l, start, stop):
            T.matmul(bank, w_h, x_h, start=start, stop=False)
            T.matmul(bank, w_h, x_l, start=False, stop=False)
            return T.matmul(bank, w_l, x_h, start=False, stop=stop)

        def project(slot, h, ks, bank):
            for k in ks:
                w = slice(k * P, (k + 1) * P)
                ins = three(bank, w_hi[:, slot, w], w_lo[:, slot, w], hn_hi[:, k, cols(h)], hn_lo[:, k, cols(h)],
                            k == 0, k == KT - 1)
            return ins

        pe.wait_ge(c_loaded, 16 * 6)
        for n in range(2 * KT):
            if n >= 3:
                pe.wait_ge(hn_done, n - 2)
            for i in range(4):
                t = 4 * (n % 2) + i
                if n < 2:
                    pe.wait_ge(xn_done, t + 1)
                ins = T.transpose(at_ps[:, n % 3, i * P:(i + 1) * P], x_in[t][:, (n // 2) * P:(n // 2 + 1) * P], ident)
            ins.then_inc(turned, 1)
        pe.wait_ge(w_split, 1)
        pe.wait_ge(hn_done, 2 * KT)
        for h in range(2):
            project(0, h, range(KT), proj_ps[:, h, :]).then_inc(proj_full, 1)
        pe.wait_ge(z_done, 1)

        with pe.Fori(0, GROUPS) as g:
            def proj_begin(j, h):
                pe.wait_ge(w_split, g * JOBS + (j + 2))
                pe.wait_ge(proj_free, g * NPJ + (2 * j + h + 1))

            def proj(j, h):
                proj_begin(j, h)
                project((j + 1) % 2, h, range(KT), proj_ps[:, h, :]).then_inc(proj_full, 1)

            def stat(name, lhs, rhs):
                pe.wait_ge(stat_free, g * NST + stat_no[name])
                T.matmul(stat_ps[:], lhs, rhs, start=True, stop=True).then_inc(stat_full, 1)

            pe.wait_ge(group_set, g + 1)
            proj(0, 0)
            stat("dec0", wlora[0:HEAD, :], z_t[0:HEAD, 0:HALF])
            proj(0, 1)
            stat("dec1", wlora[0:HEAD, :], z_t[0:HEAD, HALF:SEQ])
            proj(1, 0)
            stat("icl0", wlora[HEAD:P, :], z_t[HEAD:P, 0:HALF])
            proj(1, 1)
            stat("icl1", wlora[HEAD:P, :], z_t[HEAD:P, HALF:SEQ])
            proj(2, 0)
            pe.wait_ge(kk_squared, g + 1)
            stat("kk0", av64, sq[:, 0:HALF])
            proj(2, 1)
            stat("kk1", av64, sq[:, HALF:SEQ])
            proj(3, 0)
            proj(3, 1)
            pe.wait_ge(rk_in, g + 1)
            stat("rk0", av64, sq[:, 0:HALF])
            proj(4, 0)
            stat("rk1", av64, sq[:, HALF:SEQ])
            proj(4, 1)
            stat("q0", av64, qk_sqs[:, 0:HALF])
            stat("q1", av64, qk_sqs[:, HALF:SEQ])

            def rk_begin(job):
                n = rk_no[job]
                pe.wait_ge(rk_free, g * NRK + max(n - 1, 0))
                settled(pe)
                return rk_ps[:, n % 2, :]

            pe.wait_ge(tildes, g + 1)
            for h in range(2):
                for a, src in enumerate((v_b, kk_b, k_b)):
                    bank = rk_begin(("turn", a, h))
                    for c in range(8):
                        for hd in range(2):
                            r = rows(hd)
                            t0 = (8 * h + c) * CH
                            ins = T.matmul(bank[r, c * CH:(c + 1) * CH], src[r, t0:t0 + CH],
                                           cst[r, C_ID + hd * HEAD:C_ID + hd * HEAD + HEAD], start=True, stop=True)
                    ins.then_inc(rk_full, 1)
            for name, src in (("ab", kk_b), ("ak", k_b)):
                for q in range(4):
                    bank = rk_begin((name, q))
                    for i in range(4):
                        c = 4 * q + i
                        for hd in range(2):
                            r = rows(hd)
                            ins = T.matmul(bank[r, i * P:(i + 1) * P], src[r, c * CH:(c + 1) * CH],
                                           ar_t[r, c, :, :].rearrange("p x t -> p (x t)"), start=True, stop=True)
                    ins.then_inc(rk_full, 1)
            proj(5, 0)
            stat("k0", av64, qk_sqs[:, 0:HALF])
            proj(5, 1)
            stat("k1", av64, qk_sqs[:, HALF:SEQ])
            proj(6, 0)

            def at_begin(job):
                n = at_no[job]
                pe.wait_ge(at_free, g * NAT + max(n - 2, 0))
                return at_ps[:, n % 3, :]

            pe.wait_ge(proj_free, g * NPJ + (4 + 2 * 5))
            for n in range(2):
                bank = at_begin(("v", n))
                for i in range(4):
                    t = 4 * n + i
                    ins = T.transpose(bank[:, i * P:(i + 1) * P], v_b[:, t * P:(t + 1) * P], ident)
                ins.then_inc(at_full, 1)
            proj(6, 1)
            pe.wait_ge(xblk_in, g * 256 + 256)
            for m, lhs, rhs in ((0, ab_m[:, :, 0, :], x_m), (1, xt_m, w_m), (2, w_m, xt_m), (3, ab_m[:, :, 0, :], x_m),
                                (4, w_m, xt_m)):
                for h in range(2):
                    bank = rk_begin(("merge", m, h))
                    for c in range(8):
                        for hd in range(2):
                            r = rows(hd)
                            ins = T.matmul(bank[r, c * CH:(c + 1) * CH], lhs[r, 8 * h + c, :], rhs[r, 8 * h + c, :],
                                           start=True, stop=True)
                    ins.then_inc(rk_full, 1)

            def pair(col, terms, bank=0):
                settled(pe)
                for hd in range(2):
                    r = rows(hd)
                    for i, (lhs, rhs) in enumerate(terms):
                        ins = T.matmul(rk_ps[r, bank, col:col + CH], lhs[r], rhs[r], start=(i == 0),
                                       stop=(i == len(terms) - 1))
                return ins

            def scores(qb, m):
                for c in range(qb // 4 + 1):
                    w = min(HALF, P * (qb + 1) - HALF * c)
                    bank = at_begin(("s", qb, m, c))
                    r = rows(m)
                    T.matmul(bank[:, 0:w], q_b[r, qb * P:(qb + 1) * P], kq_b[r, HALF * c:HALF * c + w],
                             start=True, stop=True).then_inc(at_full, 1)

            def turn_attn(qb):
                pe.wait_ge(attn_done, g * TT + (qb + 1))
                for c in range(qb // 4 + 1):
                    bank = at_begin(("t", qb, c))
                    for i in range(min(4, qb + 1 - 4 * c)):
                        ins = T.transpose(bank[:, i * P:(i + 1) * P], sc_b[:, 0, (4 * c + i) * P:(4 * c + i + 1) * P], ident)
                    ins.then_inc(at_full, 1)

            def weigh_values(qb):
                pe.wait_ge(at_free, g * NAT + (at_no["t", qb, qb // 4] + 1))
                bank = at_begin(("o", qb))
                for k in range(qb + 1):
                    ins = T.matmul(bank[:, 0:P], val[:, k, :], attn_t[:, k, :], start=(k == 0), stop=(k == qb))
                ins.then_inc(at_full, 1)

            def gate_part(n):
                h, k = n // 8, n % 8
                if k == 0:
                    proj_begin(7, h)
                ins = project(0, h, [k], proj_ps[:, h, :])
                if k == 7:
                    ins.then_inc(proj_full, 1)

            pe.wait_ge(rk_free, g * NRK + NRK)
            pe.wait_ge(qk_done, g * 2 + 2)
            for c in range(NCH):
                qb, odd = c // 2, c % 2
                pe.wait_ge(s_done, g * (NCH + 1) + (c + 1))
                pair(0, [(ak_m[:, c, 0, :], v_t[:, c, :]), (ar_t[:, c, 0, :], s_t[:, c % 2, :])]).then_inc(step_full, 1)
                if not odd:
                    if qb >= 1:
                        weigh_values(qb - 1)
                    scores(qb, 0)
                gate_part(c)
                pe.wait_ge(u0_done, g * NCH + (c + 1))
                pair(CH, [(xt_m[:, c, :], u0_t[:])]).then_inc(step_full, 1)
                if not odd:
                    scores(qb, 1)
                pe.wait_ge(u_done, g * NCH + (c + 1))
                pair(2 * CH, [(k_t[:, c, :], v_t[:, c, :]), (b_t[:, c, :], u_t[:, c % 2, :])]).then_inc(step_full, 1)
                if c % 8 == 0 and c > 0:
                    pe.wait_ge(y_out, g * 2 + c // 8)
                ins = pair((c % 8) * CH, [(s_t[:, c % 2, :], ar_t[:, c, 1, :]), (u_t[:, c % 2, :], ab_m[:, c, 1, :]),
                                          (v_t[:, c, :], ak_m[:, c, 1, :])], bank=1)
                if c % 8 == 7:
                    ins.then_inc(y_full, 1)
                if odd:
                    turn_attn(qb)
                if c == 8:
                    stat("ym0", av64, y_b[:, 0:HALF])
                if c == 10:
                    pe.wait_ge(y_sq, g * 2 + 1)
                    stat("yv0", av64, y_sqs)
                if c == 11:
                    pe.wait_ge(o_sq, g * 2 + 1)
                    stat("om0", av128, o_sqs)
            weigh_values(TT - 1)
            pe.wait_ge(y_out, g * 2 + 2)
            stat("ym1", av64, y_b[:, HALF:SEQ])
            pe.wait_ge(y_sq, g * 2 + 2)
            stat("yv1", av64, y_sqs)
            pe.wait_ge(o_sq, g * 2 + 2)
            stat("om1", av128, o_sqs)

        for s in range(4):
            for e in range(KT):
                if s == 0:
                    pe.wait_ge(m_split, e + 1)
                    pe.wait_ge(wo_split, e + 1)
                for i in range(4):
                    n = 4 * s + i
                    if e == 0 and s >= 2:
                        pe.wait_ge(out_sum, n - 7)
                    t = slice((n // 2) * P, (n // 2 + 1) * P)
                    ins = three(out_banks[n % 8], hn_hi[:, e, t], hn_lo[:, e, t], wo_hi[:, e, cols(n % 2)],
                                wo_lo[:, e, cols(n % 2)], e == 0, e == KT - 1)
                    if e == KT - 1:
                        ins.then_inc(out_full, 1)


def host_constants():
    p = np.arange(P)
    cst = np.zeros((P, C_WIDTH), np.float32)
    cst[:, C_ID:C_ID + P] = np.eye(P)
    cst[:, C_AV64:C_AV64 + P] = (p[:, None] // HEAD == p[None, :] // HEAD) / HEAD
    cst[:, C_AV128:C_AV128 + P] = 1.0 / P
    s, t = (p % CH)[:, None], np.arange(CH)[None, :]
    cst[:, C_AMASK:C_AMASK + CH] = s < t
    cst[:, C_AMASK + CH:C_AMASK + 2 * CH] = s <= t
    row, col = s, t
    cst[:, C_M1:C_M1 + CH] = ((row // 32) == (col // 32)) & ((row // 16) % 2 == 1) & ((col // 16) % 2 == 0)
    cst[:, C_M2:C_M2 + CH] = (row >= 32) & (col < 32)
    cst[:, C_EYE:C_EYE + BLK] = np.eye(SUB).reshape(1, BLK)
    dist = p[:, None] + (SEQ - P) - np.arange(SEQ)[None, :]
    slopes = [2.0 ** (-8.0 * (h + 1) / GROUPS) for h in range(GROUPS)]
    alibi = np.stack([np.where(dist >= 0, -sl * dist, -1e30) for sl in slopes]).astype(np.float32)
    return cst, alibi


def kernel(x, norm_g, w_in, shift_mu, w0, w_decay_up, a0, w_iclr_up, k_k, k_a, r_k, ln_x_w, ln_x_b,
           q_norm_g, k_norm_g, lambda_q1, lambda_k1, lambda_q2, lambda_k2, subln_g, w_out):
    import concourse.bacc as _bacc
    from concourse.bass_utils import run_bass_kernel_spmd as _run

    A = np.asarray
    W = GROUPS * P

    def tiles(w):
        w = A(w)
        return w.reshape(KT, P, w.shape[1] // P, P).transpose(2, 1, 0, 3).reshape(-1, P, SEQ)

    wt = tiles(A(w_in)[0])
    order = [12]
    for g in range(GROUPS):
        order += [4 + g, g, 8 + g, 17 + g, 21 + g, 25 + g, 13 + g, 29 + g]
    w_all = np.ascontiguousarray(np.concatenate([wt[order], A(w_out)[0].reshape(KT, P, D_MODEL)]))

    def per_group(v):
        return A(v).reshape(GROUPS, P).T

    mu = A(shift_mu)[0]
    prm = np.ascontiguousarray(np.stack([per_group(v) for v in (
        mu[0:W], mu[W:2 * W], mu[2 * W:3 * W], A(w0)[0], A(a0)[0], A(k_k)[0], A(k_a)[0], A(r_k)[0],
        A(ln_x_w)[0], A(ln_x_b)[0])], axis=2))
    qg, kg = A(q_norm_g)[0], A(k_norm_g)[0]
    shared = np.ascontiguousarray(np.stack([mu[3 * W:], np.tile(qg, 2), np.tile(kg, 2), A(subln_g)[0]], axis=1))
    lam_in = np.ascontiguousarray(np.broadcast_to(
        np.stack([A(lambda_q1)[0], A(lambda_q2)[0], A(lambda_k1)[0], A(lambda_k2)[0]])[None], (P, 4, HEAD)))
    ng = np.ascontiguousarray(A(norm_g)[0].reshape(KT, P).T)
    w_lora = np.ascontiguousarray(
        np.concatenate([A(w_decay_up)[0], A(w_iclr_up)[0]]).reshape(P, GROUPS, P))
    cst, alibi = host_constants()
    arrays = {"x": np.ascontiguousarray(A(x)[0]), "w_all": w_all, "prm": prm, "shared": shared, "lam_in": lam_in,
              "norm_g": ng, "w_lora": w_lora, "consts": cst, "alibi": alibi}
    nc = _bacc.Bacc("TRN2", target_bir_lowering=False, num_devices=1)
    args = [nc.dram_tensor(n, a.shape, F32, kind="ExternalInput").ap() for n, a in arrays.items()]
    args.append(nc.dram_tensor("out", (SEQ, D_MODEL), F32, kind="ExternalOutput").ap())
    for n, s in (("mixed", (KT, P, SEQ)), ("nblk_d", (8, NCH, SUB, SUB)), ("xblk_d", (2, 8, NCH, SUB, SUB))):
        args.append(nc.dram_tensor(n, s, F32, kind="Internal").ap())
    with ExitStack() as ctx:
        build(nc, ctx, *args)
    r = _run(nc, [arrays], core_ids=[0])
    return r.results[0]["out"].reshape(1, SEQ, D_MODEL)
```

```python
from contextlib import ExitStack

import numpy as np
import concourse.bass as bass
from concourse import mybir

F32 = mybir.dt.float32
F32R = mybir.dt.float32r
ALU = mybir.AluOpType
ACT = mybir.ActivationFunctionType
AX_X = mybir.AxisListType.X

P = 128
SEQ = 1024
D_MODEL = 1024
KT = D_MODEL // P
TT = SEQ // P
HALF = 512
GROUPS = 4
HEAD = 64
CH = 64
NCH = SEQ // CH
SUB = 16
BLK = SUB * SUB
JOBS = 8
DECAY_MAX = float(np.exp(-0.5))
NORM_EPS = 1e-6
GN_EPS = 64e-5
SUBLN_EPS = 1e-5
LAMBDA_INIT = 0.8 - 0.6
PAD = 4

MU_R, MU_K, MU_V, W0, A0, K_K, K_A, R_K, LN_W, LN_B = range(10)
N_PRM = 10
OM_R, OM_K, OM_V, OM_KA, HALF_W0, HALF_A0 = range(10, 16)
N_DER = 16
MU_Z, Q_G, K_G, SUB_G, OM_Z, Q_GS, SUB_GS = range(7)
C_ID, C_AV64, C_AV128, C_AMASK, C_M1, C_M2, C_EYE = 0, 128, 256, 384, 512, 576, 640
C_WIDTH = 640 + BLK


def build(nc, ctx, x, w_all, prm, shared, lam_in, norm_g, w_lora, consts, alibi, out,
          mixed_dram, nblk_dram, xblk_dram):

    def sem(name):
        return ctx.enter_context(nc.semaphore(name))

    def sb(name, shape, dt=F32):
        return ctx.enter_context(nc.sbuf_tensor(name, shape, dt))

    proj_ps = ctx.enter_context(nc.psum_tensor("proj_ps", [P, 2, HALF], F32))
    stat_ps = ctx.enter_context(nc.psum_tensor("stat_ps", [P, HALF], F32))
    rk_ps = ctx.enter_context(nc.psum_tensor("rk_ps", [P, 2, HALF], F32))
    at_ps = ctx.enter_context(nc.psum_tensor("at_ps", [P, 3, HALF], F32))

    hn_hi = sb("hn_hi", [P, KT, SEQ], F32R)
    hn_lo = sb("hn_lo", [P, KT, SEQ], F32R)
    w_raw = sb("w_raw", [P, 2, SEQ])
    w_hi = sb("w_hi", [P, 2, SEQ], F32R)
    w_lo = sb("w_lo", [P, 2, SEQ], F32R)
    cst = sb("cst", [P, C_WIDTH])
    ident = cst[:, C_ID:C_ID + P]
    av64 = cst[:, C_AV64:C_AV64 + P]
    av128 = cst[:, C_AV128:C_AV128 + P]
    eps = sb("eps", [P, 4])
    zero_t = sb("zero_t", [P, CH])
    out_banks = [proj_ps[:, 0, :], proj_ps[:, 1, :], rk_ps[:, 0, :], rk_ps[:, 1, :],
                 at_ps[:, 0, :], at_ps[:, 1, :], at_ps[:, 2, :], stat_ps[:]]
    amask = cst[:, C_AMASK:C_AMASK + 2 * CH]
    m1mask = cst[:, C_M1:C_M1 + CH]
    m2mask = cst[:, C_M2:C_M2 + CH]

    loop_mem = ExitStack()

    def lb(name, shape, dt=F32):
        return loop_mem.enter_context(nc.sbuf_tensor(name, shape, dt))

    prm_all = lb("prm_all", [P, GROUPS + 1, N_DER])
    shr = lb("shr", [P, 8])
    ng = lb("ng", [P, KT])
    small = lb("small", [P, 32])
    cur = lb("cur", [P, N_DER])
    ln_wb = lb("ln_wb", [P, 2])
    wlora = lb("wlora", [P, P])
    z_t = lb("z_t", [P, SEQ])
    shift_raw = lb("shift_raw", [P, PAD + SEQ])
    bias_t = lb("bias_t", [P, SEQ])
    k_b = lb("k_b", [P, SEQ])
    r_b = lb("r_b", [P, SEQ])
    v_b = lb("v_b", [P, SEQ])
    kk_b = lb("kk_b", [P, SEQ])
    bonus = lb("bonus", [P, SEQ])
    ar_t = lb("ar_t", [P, NCH, 2, CH])
    work = lb("work", [P, 7, SEQ])
    v_t = lb("v_t", [P, NCH, CH])
    b_t = lb("b_t", [P, NCH, CH])
    k_t = lb("k_t", [P, NCH, CH])
    s_t = lb("s_t", [P, 2, CH])
    sp_t = lb("sp_t", [P, CH])
    u0_t = lb("u0_t", [P, CH])
    u_t = lb("u_t", [P, 2, CH])
    pc = lb("pc", [P, NCH])
    q_z = lb("q_z", [P, 2, SEQ])
    kq_b = lb("kq_b", [P, SEQ])
    val = lb("val", [P, TT, P])
    sc_b = lb("sc_b", [P, 2, SEQ])
    attn_t = lb("attn_t", [P, TT, P])
    o_b = lb("o_b", [P, SEQ])

    lw, cc, aa, e1, ex, sq, nrm = (work[:, i, :] for i in range(7))
    ab_m = work[:, 0:2, :].rearrange("p a (c x t) -> p (a c) x t", x=2, t=CH)
    ak_m = work[:, 2:4, :].rearrange("p a (c x t) -> p (a c) x t", x=2, t=CH)
    x_m = work[:, 4, :].rearrange("p (c t) -> p c t", t=CH)
    xt_m = work[:, 5, :].rearrange("p (c t) -> p c t", t=CH)
    w_m = work[:, 6, :].rearrange("p (c t) -> p c t", t=CH)
    nblk = work[:, 6, 0:BLK].rearrange("p (s t) -> p s t", t=SUB)
    xblk = work[:, 6, BLK:2 * BLK].rearrange("p (t s) -> p t s", s=SUB)
    xblkt = work[:, 6, 2 * BLK:3 * BLK].rearrange("p (s t) -> p s t", t=SUB)
    prod = work[:, 6, 3 * BLK:4 * BLK].rearrange("p (t s) -> p t s", s=SUB)
    x_in = [k_b, r_b, v_b, kk_b, bonus, ar_t[:, 0:8, :, :].rearrange("p c x t -> p (c x t)"), kq_b, o_b]
    ga_b, gb_b = r_b, kk_b
    mx, nm, ls, rl, c1 = small[:, 0:4], small[:, 4:6], small[:, 6:8], small[:, 8:10], small[:, 10:11]
    lam_neg = small[:, 11:12]
    ssq, rstd = small[:, 12:20], small[:, 20:28]
    lam_dot, lam_e = small[:, 28:30], small[:, 30:32]
    lam_sb = work[:, 2, 0:4 * HEAD].rearrange("p (a b) -> p a b", b=HEAD)
    x_scr = [work[:, 0, :], work[:, 1, :]]
    y_half = [k_b[:, 0:HALF], kq_b[:, 0:HALF]]
    y_sqs, y_nrm = v_b[:, 0:HALF], v_b[:, HALF:SEQ]
    o_sqs, o_nrm = work[:, 6, 0:HALF], work[:, 6, HALF:SEQ]
    ga_th, gb_th = o_b, shift_raw[:, PAD:PAD + SEQ]
    q_raw = o_b
    q_sqs, k_sqs = sc_b[:, 0, :], sc_b[:, 1, :]
    q_nrm, k_nrm = val.rearrange("p a b -> p (a b)"), attn_t.rearrange("p a b -> p (a b)")


    loop_mem.close()
    wo_hi = sb("wo_hi", [P, KT, SEQ], F32R)
    wo_lo = sb("wo_lo", [P, KT, SEQ], F32R)
    m_raw = sb("m_raw", [P, 2, SEQ])
    x_res = sb("x_res", [P, 2, SEQ])
    o_stage = sb("o_stage", [P, 2, SEQ])

    c_loaded = sem("c_loaded")
    x_loaded = [sem(f"x_loaded{t}") for t in range(TT)]
    w_loaded = [sem("w_loaded0"), sem("w_loaded1")]
    w_hi_done, w_split = sem("w_hi_done"), sem("w_split")
    proj_full, proj_free = sem("proj_full"), sem("proj_free")
    ssq_done, xn_done = sem("ssq_done"), sem("xn_done")
    turned, hi_done, hn_done = sem("turned"), sem("hi_done"), sem("hn_done")
    prm_done, lam_exp, z_shifted, z_done = sem("prm_done"), sem("lam_exp"), sem("z_shifted"), sem("z_done")
    group_set, wlora_in = sem("group_set"), sem("wlora_in")
    shifted = sem("shifted")
    stat_full, stat_free = sem("stat_full"), sem("stat_free")
    kk_squared, rk_in = sem("kk_squared"), sem("rk_in")
    scanned, exps_done = sem("scanned"), sem("exps_done")
    tildes = sem("tildes")
    turn_full, turn_free = sem("turn_full"), sem("turn_free")
    qk_scaled = sem("qk_scaled")
    qk_done = sem("qk_done")
    rk_full, rk_free = sem("rk_full"), sem("rk_free")
    nblk_out, nblk_in = sem("nblk_out"), sem("nblk_in")
    blocks_done, xblk_out, xblk_in = sem("blocks_done"), sem("xblk_out"), sem("xblk_in")
    x_zeroed = sem("x_zeroed")
    step_full = sem("step_full")
    u0_done, u_done, s_done = sem("u0_done"), sem("u_done"), sem("s_done")
    y_full, y_out = sem("y_full"), sem("y_out")
    y_sq, y_fin = sem("y_sq"), sem("y_fin")
    at_full, at_free = sem("at_full"), sem("at_free")
    weights_out = sem("weights_out")
    neg_done, exp_done, attn_done = sem("neg_done"), sem("exp_done"), sem("attn_done")
    o_sq, o_fin = sem("o_sq"), sem("o_fin")
    y_scaled, o_scaled = sem("y_scaled"), sem("o_scaled")
    bias_in, mixed_out = sem("bias_in"), sem("mixed_out")
    m_in = [sem("m_in0"), sem("m_in1")]
    m_hi_done, m_split = sem("m_hi_done"), sem("m_split")
    wo_hi_done, wo_split = sem("wo_hi_done"), sem("wo_split")
    res_in = [sem("res_in0"), sem("res_in1")]
    out_full, out_sum = sem("out_full"), sem("out_sum")
    stored = [sem("stored0"), sem("stored1")]

    FROM = 1
    from_one = [stat_free, rk_free, at_free, y_fin, o_fin, mixed_out]
    STATS = ["dec0", "dec1", "icl0", "icl1", "kk0", "kk1", "q0", "q1", "rk0", "rk1", "k0", "k1",
             "ym0", "yv0", "om0", "ym1", "yv1", "om1"]
    NST = len(STATS)
    stat_no = {s: n for n, s in enumerate(STATS)}
    TURNS = [(a, h) for a in range(3) for h in range(2)]
    NTURN = len(TURNS)
    RK_JOBS = ([("ab", q) for q in range(4)] + [("ak", q) for q in range(4)]
               + [("merge", m, h) for m in range(5) for h in range(2)])
    NRK = len(RK_JOBS)
    rk_no = {j: n for n, j in enumerate(RK_JOBS)}
    AT_JOBS = [("v", 0), ("v", 1)]
    for qb in range(TT):
        nh = qb // 4 + 1
        if qb >= 1:
            AT_JOBS += [("t", qb - 1, c) for c in range((qb - 1) // 4 + 1)]
        AT_JOBS += [("s", qb, m, c) for m in range(2) for c in range(nh)]
        if qb >= 1:
            AT_JOBS += [("o", qb - 1)]
    AT_JOBS += [("t", TT - 1, c) for c in range(2)] + [("o", TT - 1)]
    NAT = len(AT_JOBS)
    at_no = {j: n for n, j in enumerate(AT_JOBS)}
    on_act = [j for j in AT_JOBS if j[0] == "t"]
    on_dve = [j for j in AT_JOBS if j[0] != "t"]
    NTA, NAD = len(on_act), len(on_dve)

    def at_freed(g, job):
        if job[0] == "t":
            return weights_out, g * NTA + (on_act.index(job) + 1)
        return at_free, g * NAD + (on_dve.index(job) + 1 + FROM)
    NPJ = 2 * JOBS
    NSTEP = 3 * NCH

    GATE_PARTS = [1, 1, 1, 1, 1, 2, 2, 2, 2, 2, 1, 1]

    def cols(h):
        return slice(h * HALF, (h + 1) * HALF)

    def rows(h):
        return slice(h * HEAD, (h + 1) * HEAD)

    passed = {e.engine: sem(f"passed{i}") for i, e in enumerate((nc.tensor, nc.vector, nc.gpsimd, nc.sync))}

    def settled(eng):
        eng.sem_inc(passed[eng.engine], 1)

    block = ctx.enter_context(nc.Block())

    @block.sync
    def _(sp):
        for s in from_one:
            sp.sem_inc(s, FROM)
        for t in range(TT):
            sp.dma_start(x_in[t][:], x[t * P:(t + 1) * P, :]).then_inc(x_loaded[t], 16)
        sp.dma_start(cst[:], consts).then_inc(c_loaded, 16)
        sp.dma_start(prm_all[:, 0:GROUPS, 0:N_PRM], prm).then_inc(c_loaded, 16)
        sp.dma_start(shr[:, 0:4], shared).then_inc(c_loaded, 16)
        sp.dma_start(ng[:], norm_g).then_inc(c_loaded, 16)
        sp.dma_start(lam_sb, lam_in).then_inc(c_loaded, 16)
        sp.dma_start(wlora[:], w_lora[0]).then_inc(wlora_in, 16)
        for j in range(2):
            sp.dma_start(w_raw[:, j, :], w_all[j]).then_inc(w_loaded[j], 16)
        sp.wait_ge(w_split, 1)
        sp.dma_start(w_raw[:, 0, :], w_all[2]).then_inc(w_loaded[0], 16)
        with sp.Fori(0, GROUPS) as g:
            sp.wait_ge(at_free, g * NAD + FROM)
            settled(sp)
            sp.dma_start(bias_t[:], alibi[bass.ds(g, 1)].rearrange("o p c -> (o p) c")).then_inc(bias_in, 16)
            for j in range(JOBS):
                sp.wait_ge(w_split, g * JOBS + (j + 2))
                sp.dma_start(w_raw[:, (j + 1) % 2, :],
                             w_all[bass.ds(g * JOBS + (j + 3), 1)].rearrange("o p c -> (o p) c")
                             ).then_inc(w_loaded[(j + 1) % 2], 16)
                if j == 2:
                    sp.wait_ge(stat_free, g * NST + (stat_no["icl1"] + 1 + FROM))
                    sp.dma_start(wlora[:], w_lora[bass.ds(g + 1, 1)].rearrange("o p n -> (o p) n")).then_inc(wlora_in, 16)
                if j == 4:
                    sp.wait_ge(rk_free, g * NRK + (rk_no["ab", 3] + 1 + FROM))
                    for i in range(8):
                        sp.dma_start(nblk_dram[i].rearrange("c s t -> s c t"),
                                     ab_m[SUB * i:SUB * i + SUB, :, 0, SUB * (i % 4):SUB * (i % 4) + SUB]
                                     ).then_inc(nblk_out, 16)
                    sp.wait_ge(nblk_out, g * 128 + 128)
                    settled(sp)
                    sp.wait_ge(tildes, g + 1)
                    sp.dma_start(nblk, nblk_dram.rearrange("i c s t -> (i c) s t")).then_inc(nblk_in, 16)
                if j == 5:
                    sp.wait_ge(blocks_done, g + 1)
                    sp.dma_start(xblk_dram[0].rearrange("i c t s -> (i c) t s"), xblk).then_inc(xblk_out, 16)
                    sp.dma_start(xblk_dram[1].rearrange("i c t s -> (i c) t s"), xblkt).then_inc(xblk_out, 16)
                    sp.wait_ge(xblk_out, g * 32 + 32)
                    sp.wait_ge(x_zeroed, g + 1)
                    for n, dst in ((0, x_m), (1, xt_m)):
                        for i in range(8):
                            sp.dma_start(dst[SUB * i:SUB * i + SUB, :, SUB * (i % 4):SUB * (i % 4) + SUB],
                                         xblk_dram[n, i].rearrange("c t s -> t c s")).then_inc(xblk_in, 16)
            sp.wait_ge(o_fin, g * 2 + (2 + FROM))
            sp.dma_start(mixed_dram[bass.ds(g + GROUPS, 1)].rearrange("o p c -> (o p) c"), o_b[:]).then_inc(mixed_out, 16)
            sp.wait_ge(y_fin, g * 2 + (2 + FROM))
            sp.dma_start(mixed_dram[bass.ds(g, 1)].rearrange("o p c -> (o p) c"), bonus[:]).then_inc(mixed_out, 16)
        sp.wait_ge(mixed_out, 32 * GROUPS + FROM)
        sp.wait_ge(wlora_in, 16 * (GROUPS + 1))
        for e in range(KT):
            if e >= 2:
                sp.wait_ge(m_split, e - 1)
            sp.dma_start(m_raw[:, e % 2, :], mixed_dram[e]).then_inc(m_in[e % 2], 16)
            if e >= 2:
                sp.wait_ge(wo_split, e - 1)
                sp.dma_start(w_raw[:, (e + 1) % 2, :], w_all[GROUPS * JOBS + 1 + e]).then_inc(w_loaded[(e + 1) % 2], 16)
        for t in range(TT):
            if t >= 2:
                sp.wait_ge(out_sum, 2 * t - 2)
            sp.dma_start(x_res[:, t % 2, :], x[t * P:(t + 1) * P, :]).then_inc(res_in[t % 2], 16)
            if t >= 1:
                sp.wait_ge(out_sum, 2 * t)
                sp.dma_start(out[(t - 1) * P:t * P, :], o_stage[:, (t - 1) % 2, :]).then_inc(stored[(t - 1) % 2], 16)
        sp.wait_ge(out_sum, 2 * TT)
        sp.dma_start(out[(TT - 1) * P:TT * P, :], o_stage[:, (TT - 1) % 2, :]).then_inc(stored[(TT - 1) % 2], 16)
        for s in stored:
            sp.wait_ge(s, 16 * TT // 2)

    @block.gpsimd
    def _(pool):
        for n in range(2):
            pool.wait_ge(w_hi_done, n + 1)
            nc.gpsimd.tensor_tensor(w_lo[:, n, :], w_raw[:, n, :], w_hi[:, n, :].bitcast(F32),
                                    ALU.subtract).then_inc(w_split, 1)
        with pool.Fori(0, GROUPS) as g:
            for j in range(JOBS):
                if j == 5:
                    pool.wait_ge(stat_free, g * NST + (stat_no["rk1"] + 1 + FROM))
                    settled(pool)
                    nc.gpsimd.memset(work[:, 4:6, :], 0.0).then_inc(x_zeroed, 1)
                pool.wait_ge(w_hi_done, g * JOBS + (j + 3))
                nc.gpsimd.tensor_tensor(w_lo[:, j % 2, :], w_raw[:, j % 2, :], w_hi[:, j % 2, :].bitcast(F32),
                                        ALU.subtract).then_inc(w_split, 1)
        for e in range(KT):
            pool.wait_ge(wo_hi_done, e + 1)
            nc.gpsimd.tensor_tensor(wo_lo[:, e, :], w_raw[:, (e + 1) % 2, :], wo_hi[:, e, :].bitcast(F32),
                                    ALU.subtract).then_inc(wo_split, 1)

    @block.scalar
    def _(act):
        for t in range(TT):
            act.wait_ge(x_loaded[t], 16)
            if t >= 2:
                act.drain()
            nc.scalar.activation(x_scr[t % 2], x_in[t][:], ACT.Square, accum_out=ssq[:, t:t + 1])
        act.drain()
        act.wait_ge(prm_done, 1)
        nc.scalar.activation(rstd, ssq, ACT.Sqrt, scale=1.0 / D_MODEL, bias=eps[:, 0:1]).then_inc(ssq_done, 1)
        nc.scalar.activation(lam_e, lam_dot, ACT.Exp).then_inc(lam_exp, 1)
        for n in range(2):
            act.wait_ge(w_loaded[n], 16)
            nc.scalar.activation(w_hi[:, n, :], w_raw[:, n, :], ACT.Copy).then_inc(w_hi_done, 1)
        for n in range(2 * KT):
            act.wait_ge(turned, n + 1)
            nc.scalar.activation(hn_hi[:, n // 2, cols(n % 2)], at_ps[:, n % 3, :], ACT.Copy,
                                 scale=ng[:, n // 2:n // 2 + 1]).then_inc(hi_done, 1)
        for h in range(2):
            act.wait_ge(proj_full, h + 1)
            nc.scalar.activation(shift_raw[:, PAD + h * HALF:PAD + (h + 1) * HALF], proj_ps[:, h, :], ACT.Copy)
            nc.scalar.activation(z_t[:, cols(h)], proj_ps[:, h, :], ACT.Copy,
                                 scale=shr[:, OM_Z:OM_Z + 1]).then_inc(proj_free, 1)
        act.wait_ge(z_shifted, 1)
        nc.scalar.activation(z_t[0:HEAD, :], z_t[0:HEAD, :], ACT.Tanh).then_inc(z_done, 1)

        with act.Fori(0, GROUPS) as g:
            def next_hi(j):
                act.wait_ge(w_loaded[j % 2], g * 64 + 16 * (j // 2 + 2))
                act.wait_ge(proj_full, g * NPJ + (2 + 2 * j))
                nc.scalar.activation(w_hi[:, j % 2, :], w_raw[:, j % 2, :], ACT.Copy).then_inc(w_hi_done, 1)

            def take_shifted(j, h, dst, om):
                act.wait_ge(proj_full, g * NPJ + (3 + 2 * j + h))
                nc.scalar.activation(shift_raw[:, PAD + h * HALF:PAD + (h + 1) * HALF], proj_ps[:, h, :], ACT.Copy)
                nc.scalar.activation(dst[:, cols(h)], proj_ps[:, h, :], ACT.Copy,
                                     scale=cur[:, om:om + 1]).then_inc(proj_free, 1)

            def take_two(j, h, dst, dst2, func, scale):
                act.wait_ge(proj_full, g * NPJ + (3 + 2 * j + h))
                nc.scalar.activation(dst[:, cols(h)], proj_ps[:, h, :], ACT.Copy)
                nc.scalar.activation(dst2[:, cols(h)], proj_ps[:, h, :], func, scale=scale).then_inc(proj_free, 1)

            def stat_to(name, dst, func, scale=1.0, bias=0.0):
                act.wait_ge(stat_full, g * NST + (stat_no[name] + 1))
                nc.scalar.activation(dst, stat_ps[:], func, scale=scale, bias=bias).then_inc(stat_free, 1)

            half_w0, half_a0 = cur[:, HALF_W0:HALF_W0 + 1], cur[:, HALF_A0:HALF_A0 + 1]
            next_hi(0)
            act.wait_ge(group_set, g + 1)
            stat_to("dec0", lw[:, 0:HALF], ACT.Tanh, 0.5, half_w0)
            take_shifted(0, 0, k_b, OM_K)
            stat_to("dec1", lw[:, HALF:SEQ], ACT.Tanh, 0.5, half_w0)
            take_shifted(0, 1, k_b, OM_K)
            next_hi(1)
            act.wait_ge(shifted, g * 3 + 1)
            nc.scalar.activation(sq, k_b[:], ACT.Square, scale=cur[:, K_K:K_K + 1]).then_inc(kk_squared, 1)
            act.wait_ge(o_fin, g * 2 + FROM)
            act.wait_ge(y_fin, g * 2 + FROM)
            stat_to("icl0", aa[:, 0:HALF], ACT.Tanh, 0.5, half_a0)
            take_shifted(1, 0, r_b, OM_R)
            stat_to("icl1", aa[:, HALF:SEQ], ACT.Tanh, 0.5, half_a0)
            take_shifted(1, 1, r_b, OM_R)
            next_hi(2)
            stat_to("kk0", nrm[:, 0:HALF], ACT.Sqrt, float(HEAD))
            stat_to("kk1", nrm[:, HALF:SEQ], ACT.Sqrt, float(HEAD))
            act.wait_ge(scanned, g + 1)
            nc.scalar.activation(e1, cc, ACT.Exp)
            nc.scalar.activation(ex, ex, ACT.Exp)
            act.drain()
            nc.scalar.activation(cc, cc, ACT.Exp, scale=-1.0).then_inc(exps_done, 1)
            act.wait_ge(shifted, g * 3 + 2)
            take_shifted(2, 0, v_b, OM_V)
            take_shifted(2, 1, v_b, OM_V)
            next_hi(3)
            act.wait_ge(mixed_out, g * 32 + FROM)
            for h in range(2):
                take_two(3, h, q_raw, q_sqs, ACT.Square, 1.0)
            next_hi(4)
            for h in range(2):
                stat_to(f"q{h}", q_nrm[:, cols(h)], ACT.Ln, 1.0, eps[:, 0:1])
            act.drain()
            nc.scalar.activation(q_nrm, q_nrm, ACT.Exp, scale=-0.5).then_inc(qk_scaled, 1)
            take_two(4, 0, kq_b, k_sqs, ACT.Square, 1.0)

            def turned_out(n):
                a, h = TURNS[n]
                act.wait_ge(turn_full, g * NTURN + (n + 1))
                nc.scalar.activation((v_t, b_t, k_t)[a][:, 8 * h:8 * h + 8, :],
                                     at_ps[:, n % 3, :].rearrange("p (c d) -> p c d", d=CH), ACT.Copy
                                     ).then_inc(turn_free, 1)

            def value_out(h):
                act.wait_ge(proj_full, g * NPJ + (3 + 2 * 5 + h))
                nc.scalar.activation(v_b[:, cols(h)], proj_ps[:, h, :], ACT.Copy).then_inc(proj_free, 1)

            for n in range(3):
                turned_out(n)
            take_two(4, 1, kq_b, k_sqs, ACT.Square, 1.0)
            next_hi(5)
            turned_out(3)
            turned_out(4)
            turned_out(5)
            act.wait_ge(stat_free, g * NST + (stat_no["rk1"] + 1 + FROM))
            for h in range(2):
                stat_to(f"k{h}", k_nrm[:, cols(h)], ACT.Ln, 1.0, eps[:, 0:1])
                value_out(h)
            act.drain()
            nc.scalar.activation(k_nrm, k_nrm, ACT.Exp, scale=-0.5).then_inc(qk_scaled, 1)
            next_hi(6)
            act.wait_ge(qk_done, g * 2 + 1)
            for h in range(2):
                take_two(6, h, r_b, ga_th, ACT.Tanh, 0.5)
            next_hi(7)

            def y_square(h):
                act.wait_ge(stat_free, g * NST + (stat_no[f"ym{h}"] + 1 + FROM))
                nc.scalar.activation(y_sqs, y_half[h], ACT.Square).then_inc(y_sq, 1)

            def o_square(h):
                act.wait_ge(*at_freed(g, ("o", 4 * h + 3)))
                nc.scalar.activation(o_sqs, o_b[:, cols(h)], ACT.Square).then_inc(o_sq, 1)

            def y_log(h):
                act.wait_ge(y_fin, g * 2 + (h + FROM))
                stat_to(f"yv{h}", y_nrm, ACT.Ln, 1.0, eps[:, 1:2])

            def inverse_roots(h):
                act.wait_ge(o_fin, g * 2 + (h + FROM))
                stat_to(f"om{h}", o_nrm, ACT.Ln, 1.0, eps[:, 2:3])
                act.drain()
                nc.scalar.activation(y_nrm, y_nrm, ACT.Exp, scale=-0.5).then_inc(y_scaled, 1)
                nc.scalar.activation(o_nrm, o_nrm, ACT.Exp, scale=-0.5).then_inc(o_scaled, 1)

            def weights_turned(qb):
                for c in range(qb // 4 + 1):
                    n = at_no["t", qb, c]
                    w = min(4, qb + 1 - 4 * c)
                    act.wait_ge(at_full, g * NAT + (n + 1))
                    nc.scalar.activation(attn_t[:, 4 * c:4 * c + w, :],
                                         at_ps[:, n % 3, 0:w * P].rearrange("p (a d) -> p a d", d=P), ACT.Copy
                                         ).then_inc(weights_out, 1)

            for c in range(0, NCH, 2):
                qb = c // 2
                if qb >= 1:
                    weights_turned(qb - 1)
                act.wait_ge(neg_done, g * TT + (qb + 1))
                for m in range(2):
                    ins = nc.scalar.activation(sc_b[:, m, 0:P * (qb + 1)], sc_b[:, m, 0:P * (qb + 1)], ACT.Exp,
                                               bias=nm[:, m:m + 1], accum_out=ls[:, m:m + 1])
                ins.then_inc(exp_done, 1)
                if c == 8:
                    take_two(7, 0, gb_b, gb_th, ACT.Tanh, 0.5)
                    y_square(0)
                if c == 12:
                    take_two(7, 1, gb_b, gb_th, ACT.Tanh, 0.5)
                if c == 10:
                    o_square(0)
                if c == 12:
                    y_log(0)
                if c == 14:
                    inverse_roots(0)
            weights_turned(TT - 1)
            y_square(1)
            o_square(1)
            y_log(1)
            inverse_roots(1)

        act.wait_ge(mixed_out, 32 * GROUPS + FROM)
        act.wait_ge(proj_full, GROUPS * NPJ + 2)
        for e in range(KT):
            act.wait_ge(m_in[e % 2], 16 * (e // 2 + 1))
            nc.scalar.activation(hn_hi[:, e, :], m_raw[:, e % 2, :], ACT.Copy).then_inc(m_hi_done, 1)
            s = (e + 1) % 2
            act.wait_ge(w_loaded[s], 16 * ((GROUPS * JOBS + 1 + e) // 2 + 1))
            nc.scalar.activation(wo_hi[:, e, :], w_raw[:, s, :], ACT.Copy).then_inc(wo_hi_done, 1)

    @block.vector
    def _(dve):
        V = nc.vector

        def affine(dst, src, a, b):
            return V.tensor_scalar(dst, src, a, b, ALU.mult, ALU.add)

        V.memset(shift_raw[:, 0:PAD], 0.0)
        V.memset(zero_t[:], 0.0)
        V.memset(eps[:, 0:1], NORM_EPS)
        V.memset(eps[:, 1:2], GN_EPS)
        V.memset(eps[:, 2:3], SUBLN_EPS)
        V.memset(prm_all[:, GROUPS, :], 0.0)
        V.memset(q_z[rows(1), 0, :], 0.0)
        V.memset(q_z[rows(0), 1, :], 0.0)
        dve.wait_ge(c_loaded, 16 * 5)
        affine(prm_all[:, 0:GROUPS, OM_R:OM_V + 1], prm_all[:, 0:GROUPS, MU_R:MU_V + 1], -1.0, 1.0)
        affine(prm_all[:, 0:GROUPS, OM_KA:OM_KA + 1], prm_all[:, 0:GROUPS, K_A:K_A + 1], -1.0, 1.0)
        V.tensor_scalar(prm_all[:, 0:GROUPS, HALF_W0:HALF_A0 + 1], prm_all[:, 0:GROUPS, W0:A0 + 1], 0.5, None, ALU.mult)
        affine(shr[:, OM_Z:OM_Z + 1], shr[:, MU_Z:MU_Z + 1], -1.0, 1.0)
        V.tensor_scalar(shr[:, Q_GS:Q_GS + 1], shr[:, Q_G:Q_G + 1], HEAD ** -0.5, None, ALU.mult)
        V.tensor_scalar(shr[:, SUB_GS:SUB_GS + 1], shr[:, SUB_G:SUB_G + 1], 1.0 - LAMBDA_INIT, None, ALU.mult)
        V.tensor_tensor(lam_sb[:, 0:2, :], lam_sb[:, 0:2, :], lam_sb[:, 2:4, :], ALU.mult)
        dve.drain()
        V.tensor_reduce(lam_dot, lam_sb[:, 0:2, :], AX_X, ALU.add).then_inc(prm_done, 1)
        dve.wait_ge(ssq_done, 1)
        V.reciprocal(rstd, rstd)
        dve.drain()
        for t in range(TT):
            V.tensor_scalar(x_in[t][:], x_in[t][:], rstd[:, t:t + 1], None, ALU.mult).then_inc(xn_done, 1)
        dve.wait_ge(lam_exp, 1)
        V.tensor_scalar(lam_neg, lam_e[:, 1:2], lam_e[:, 0:1], -LAMBDA_INIT, ALU.subtract, ALU.add)
        for n in range(2 * KT):
            dve.wait_ge(hi_done, n + 1)
            V.scalar_tensor_tensor(out=hn_lo[:, n // 2, cols(n % 2)], in0=at_ps[:, n % 3, :],
                                   scalar=ng[:, n // 2:n // 2 + 1], in1=hn_hi[:, n // 2, cols(n % 2)].bitcast(F32),
                                   op0=ALU.mult, op1=ALU.subtract).then_inc(hn_done, 1)
        dve.wait_ge(proj_free, 2)
        V.scalar_tensor_tensor(out=z_t[:], in0=shift_raw[:, PAD - 1:PAD - 1 + SEQ], scalar=shr[:, MU_Z:MU_Z + 1],
                               in1=z_t[:], op0=ALU.mult, op1=ALU.add).then_inc(z_shifted, 1)

        V.tensor_copy(cur[:], prm_all[:, 0, :])
        dve.drain().then_inc(group_set, 1)

        with dve.Fori(0, GROUPS) as g:
            def prm1(i):
                return cur[:, i:i + 1]

            def stt(dst, a, s, b, op0=ALU.mult, op1=ALU.mult):
                return V.scalar_tensor_tensor(out=dst, in0=a, scalar=s, in1=b, op0=op0, op1=op1)

            def mul(dst, a, b):
                return V.tensor_tensor(dst, a, b, ALU.mult)

            def shift(j, dst, mu):
                dve.wait_ge(proj_free, g * NPJ + (4 + 2 * j))
                stt(dst[:], shift_raw[:, PAD - 1:PAD - 1 + SEQ], prm1(mu), dst[:], ALU.mult, ALU.add).then_inc(shifted, 1)

            def rk_take(job):
                n = rk_no[job]
                dve.wait_ge(rk_full, g * NRK + (n + 1))
                return rk_ps[:, n % 2, :]

            def at_take(job):
                n = at_no[job]
                dve.wait_ge(at_full, g * NAT + (n + 1))
                return at_ps[:, n % 3, :]

            def sigmoid(buf):
                return affine(buf, buf, 0.5, 0.5)

            V.tensor_copy(ln_wb[:], cur[:, LN_W:LN_B + 1])
            shift(0, k_b, MU_K)
            dve.wait_ge(stat_free, g * NST + (2 + FROM))
            affine(lw, lw, -0.5 * DECAY_MAX, -0.5 * DECAY_MAX)
            dve.drain()
            for c in range(NCH):
                s = slice(c * CH, (c + 1) * CH)
                V.tensor_tensor_scan(cc[:, s], lw[:, s], zero_t[:], 0.0, ALU.add, ALU.add)
            dve.drain()
            V.tensor_tensor(ex, cc, lw, ALU.subtract).then_inc(scanned, 1)
            dve.wait_ge(stat_free, g * NST + (4 + FROM))
            sigmoid(aa)
            shift(1, r_b, MU_R)
            dve.drain()
            V.tensor_scalar(lw, aa, prm1(K_A), prm1(OM_KA), ALU.mult, ALU.add)
            for h in range(2):
                dve.wait_ge(stat_free, g * NST + (stat_no[f"kk{h}"] + 1 + FROM))
                V.tensor_scalar(nrm[:, cols(h)], nrm[:, cols(h)], 1e-12, None, ALU.max)
                dve.drain()
                V.reciprocal(nrm[:, cols(h)], nrm[:, cols(h)])
            dve.drain()
            stt(kk_b[:], k_b[:], prm1(K_K), nrm)
            dve.drain()
            mul(k_b[:], k_b[:], lw)
            shift(2, v_b, MU_V)
            dve.drain()
            stt(sq, r_b[:], prm1(R_K), k_b[:]).then_inc(rk_in, 1)
            dve.wait_ge(exps_done, g + 1)
            V.tensor_copy(pc[:], e1.rearrange("p (c t) -> p c t", t=CH)[:, :, CH - 1])
            ch3 = lambda ap: ap.rearrange("p (c t) -> p c t", t=CH)
            mul(ar_t[:, :, 1, :], ch3(r_b[:]), ch3(e1))
            stt(ar_t[:, :, 0, :], ch3(kk_b[:]), -1.0, ch3(ex))
            dve.drain()
            mul(kk_b[:], kk_b[:], aa)
            mul(k_b[:], k_b[:], cc)
            dve.drain()
            mul(kk_b[:], kk_b[:], cc).then_inc(tildes, 1)
            def chunk_matrices(name, dst):
                for q in range(4):
                    V.tensor_tensor(dst[:, 4 * q:4 * q + 4, :, :].rearrange("p c x t -> p c (x t)"),
                                    rk_take((name, q)).rearrange("p (c t) -> p c t", c=4),
                                    amask.unsqueeze(1).broadcast_to([P, 4, 2 * CH]), ALU.mult).then_inc(rk_free, 1)

            def qk_norm(n):
                dve.wait_ge(qk_scaled, g * 2 + (n + 1))
                if n == 0:
                    for m in range(2):
                        ins = stt(q_z[rows(m), m, :], q_raw[rows(m), :], shr[rows(m), Q_GS:Q_GS + 1], q_nrm[rows(m), :])
                else:
                    ins = stt(kq_b[:], kq_b[:], shr[:, K_G:K_G + 1], k_nrm)
                ins.then_inc(qk_done, 1)

            chunk_matrices("ab", ab_m)
            dve.wait_ge(mixed_out, g * 32 + FROM)
            for h in range(2):
                dve.wait_ge(stat_full, g * NST + (stat_no[f"rk{h}"] + 1))
                stt(bonus[:, cols(h)], stat_ps[:], float(HEAD), v_b[:, cols(h)]).then_inc(stat_free, 1)
            qk_norm(0)
            V.tensor_copy(xblk.rearrange("p t s -> p (t s)"), cst[:, C_EYE:C_EYE + BLK])
            dve.wait_ge(nblk_in, g * 16 + 16)
            settled(dve)
            for t in range(1, SUB):
                dve.drain()
                mul(prod[:, 0:t, 0:t], xblk[:, 0:t, 0:t].rearrange("p s j -> p j s"),
                    nblk[:, 0:t, t].unsqueeze(1).broadcast_to([P, t, t]))
                dve.drain()
                V.tensor_reduce(xblk[:, t, 0:t], prod[:, 0:t, 0:t], AX_X, ALU.add)
            dve.drain()
            V.tensor_copy(xblkt, xblk.rearrange("p t s -> p s t")).then_inc(blocks_done, 1)
            chunk_matrices("ak", ak_m)
            qk_norm(1)
            for n in range(2):
                V.tensor_copy(val[:, 4 * n:4 * n + 4, :], at_take(("v", n)).rearrange("p (a d) -> p a d", d=P)
                              ).then_inc(at_free, 1)
            def merged(m, h):
                return rk_take(("merge", m, h)).rearrange("p (c d) -> p c d", d=CH)

            for m, dst, mask in ((0, w_m, m1mask), (1, x_m, None), (2, xt_m, None), (3, w_m, m2mask), (4, xt_m, None)):
                for h in range(2):
                    part = dst[:, 8 * h:8 * h + 8, :]
                    if mask is not None:
                        V.tensor_tensor(part, merged(m, h), mask.unsqueeze(1).broadcast_to([P, 8, CH]),
                                        ALU.mult).then_inc(rk_free, 1)
                    else:
                        V.tensor_tensor(part, merged(m, h), part, ALU.add).then_inc(rk_free, 1)
            V.memset(s_t[:, 0, :], 0.0).then_inc(s_done, 1)

            def scores(qb, m):
                nh = qb // 4 + 1
                if qb == 0 and m == 0:
                    dve.wait_ge(bias_in, g * 16 + 16)
                for c in range(nh):
                    w = min(HALF, P * (qb + 1) - HALF * c)
                    off = SEQ - P - P * qb + HALF * c
                    bank = at_take(("s", qb, m, c))
                    settled(dve)
                    V.tensor_tensor_reduce(out=sc_b[:, m, HALF * c:HALF * c + w],
                                           in0=bank[:, 0:w], in1=bias_t[:, off:off + w],
                                           scale=1.0, scalar=-3e38, op0=ALU.add, op1=ALU.max,
                                           accum_out=mx[:, 2 * m + c:2 * m + c + 1]).then_inc(at_free, 1)

            def negate(qb):
                dve.drain()
                for m in range(2):
                    if qb < 4:
                        ins = V.tensor_scalar(nm[:, m:m + 1], mx[:, 2 * m:2 * m + 1], -1.0, None, ALU.mult)
                    else:
                        ins = V.tensor_scalar(nm[:, m:m + 1], mx[:, 2 * m:2 * m + 1], mx[:, 2 * m + 1:2 * m + 2],
                                              -1.0, ALU.max, ALU.mult)
                ins.then_inc(neg_done, 1)

            def weigh(qb):
                dve.wait_ge(exp_done, g * TT + (qb + 1))
                V.reciprocal(rl, ls)
                dve.drain()
                mul(c1, rl[:, 1:2], lam_neg)
                dve.drain()
                n = P * (qb + 1)
                V.tensor_scalar(sc_b[:, 1, 0:n], sc_b[:, 1, 0:n], c1, None, ALU.mult)

            def combine(qb):
                n = P * (qb + 1)
                dve.drain()
                stt(sc_b[:, 0, 0:n], sc_b[:, 0, 0:n], rl[:, 0:1], sc_b[:, 1, 0:n], ALU.mult, ALU.add).then_inc(attn_done, 1)

            def attn_out(qb):
                V.tensor_copy(o_b[:, P * qb:P * qb + P], at_take(("o", qb))[:, 0:P]).then_inc(at_free, 1)

            def y_take(h):
                dve.wait_ge(y_full, g * 2 + h + 1)
                V.tensor_copy(y_half[h], rk_ps[:, 1, :]).then_inc(y_out, 1)

            def y_centre(h):
                dve.wait_ge(stat_full, g * NST + (stat_no[f"ym{h}"] + 1))
                V.tensor_tensor(y_half[h], y_half[h], stat_ps[:], ALU.subtract).then_inc(stat_free, 1)

            def y_finish(h):
                dve.wait_ge(y_scaled, g * 2 + (h + 1))
                mul(y_half[h], y_half[h], y_nrm)
                dve.drain()
                affine(y_half[h], y_half[h], ln_wb[:, 0:1], ln_wb[:, 1:2])
                dve.drain()
                V.tensor_tensor(bonus[:, cols(h)], bonus[:, cols(h)], y_half[h], ALU.add)
                dve.drain()
                mul(bonus[:, cols(h)], bonus[:, cols(h)], ga_b[:, cols(h)]).then_inc(y_fin, 1)

            def gate_b(h):
                dve.wait_ge(proj_free, g * NPJ + (3 + 2 * 7 + h))
                sigmoid(gb_th[:, cols(h)])
                dve.drain()
                mul(gb_b[:, cols(h)], gb_b[:, cols(h)], gb_th[:, cols(h)])

            def gate_a():
                dve.wait_ge(proj_free, g * NPJ + (4 + 2 * 6))
                sigmoid(ga_th[:])
                dve.drain()
                mul(ga_b[:], ga_b[:], ga_th[:])

            def o_finish(h):
                dve.wait_ge(o_scaled, g * 2 + (h + 1))
                stt(o_b[:, cols(h)], o_b[:, cols(h)], shr[:, SUB_GS:SUB_GS + 1], o_nrm)
                dve.drain()
                mul(o_b[:, cols(h)], o_b[:, cols(h)], gb_b[:, cols(h)]).then_inc(o_fin, 1)

            for c in range(NCH):
                qb, odd = c // 2, c % 2
                dve.wait_ge(step_full, g * NSTEP + (3 * c + 1))
                V.tensor_copy(u0_t[:], rk_ps[:, 0, 0:CH]).then_inc(u0_done, 1)
                dve.drain()
                V.tensor_scalar(sp_t[:], s_t[:, c % 2, :], pc[:, c:c + 1], None, ALU.mult)
                if c == 8:
                    y_take(0)
                if not odd:
                    scores(qb, 0)
                else:
                    weigh(qb)
                dve.wait_ge(step_full, g * NSTEP + (3 * c + 2))
                V.tensor_copy(u_t[:, c % 2, :], rk_ps[:, 0, CH:2 * CH]).then_inc(u_done, 1)
                if not odd:
                    scores(qb, 1)
                    negate(qb)
                    if qb >= 1:
                        attn_out(qb - 1)
                else:
                    combine(qb)
                dve.wait_ge(step_full, g * NSTEP + (3 * c + 3))
                stt(s_t[:, (c + 1) % 2, :], rk_ps[:, 0, 2 * CH:3 * CH], pc[:, c:c + 1], sp_t[:], ALU.mult, ALU.add).then_inc(s_done, 1)
                if c == 8:
                    y_centre(0)
                if c == 1:
                    gate_a()
                if c == 9:
                    gate_b(0)
                if c == 13:
                    gate_b(1)
            V.tensor_copy(cur[:], prm_all[:, bass.ds(g + 1, 1), :].rearrange("p o n -> p (o n)"))
            dve.drain().then_inc(group_set, 1)
            y_take(1)
            y_centre(1)
            y_finish(0)
            attn_out(TT - 1)
            o_finish(0)
            y_finish(1)
            o_finish(1)

        for e in range(KT):
            dve.wait_ge(m_hi_done, e + 1)
            V.tensor_tensor(hn_lo[:, e, :], m_raw[:, e % 2, :], hn_hi[:, e, :].bitcast(F32), ALU.subtract).then_inc(m_split, 1)
        for t in range(TT):
            dve.wait_ge(res_in[t % 2], 16 * (t // 2 + 1))
            if t >= 2:
                dve.wait_ge(stored[t % 2], 16 * (t // 2))
            for h in range(2):
                n = 2 * t + h
                dve.wait_ge(out_full, n + 1)
                V.tensor_tensor(o_stage[:, t % 2, cols(h)], out_banks[n % 8], x_res[:, t % 2, cols(h)], ALU.add).then_inc(out_sum, 1)

    @block.tensor
    def _(pe):
        T = nc.tensor

        def three(bank, w_h, w_l, x_h, x_l, start, stop):
            T.matmul(bank, w_h, x_h, start=start, stop=False)
            T.matmul(bank, w_h, x_l, start=False, stop=False)
            return T.matmul(bank, w_l, x_h, start=False, stop=stop)

        def project(slot, h, ks, bank):
            for k in ks:
                w = slice(k * P, (k + 1) * P)
                ins = three(bank, w_hi[:, slot, w], w_lo[:, slot, w], hn_hi[:, k, cols(h)], hn_lo[:, k, cols(h)],
                            k == 0, k == KT - 1)
            return ins

        pe.wait_ge(c_loaded, 16 * 5)
        for n in range(2 * KT):
            if n >= 3:
                pe.wait_ge(hn_done, n - 2)
            for i in range(4):
                t = 4 * (n % 2) + i
                if n < 2:
                    pe.wait_ge(xn_done, t + 1)
                ins = T.transpose(at_ps[:, n % 3, i * P:(i + 1) * P], x_in[t][:, (n // 2) * P:(n // 2 + 1) * P], ident)
            ins.then_inc(turned, 1)
        pe.wait_ge(w_split, 1)
        pe.wait_ge(hn_done, 2 * KT)
        for h in range(2):
            project(0, h, range(KT), proj_ps[:, h, :]).then_inc(proj_full, 1)
        pe.wait_ge(z_done, 1)

        with pe.Fori(0, GROUPS) as g:
            def proj_begin(j, h):
                pe.wait_ge(w_split, g * JOBS + (j + 2))
                pe.wait_ge(proj_free, g * NPJ + (2 * j + h + 1))

            def proj(j, h):
                proj_begin(j, h)
                project((j + 1) % 2, h, range(KT), proj_ps[:, h, :]).then_inc(proj_full, 1)

            def stat(name, lhs, rhs):
                pe.wait_ge(stat_free, g * NST + (stat_no[name] + FROM))
                T.matmul(stat_ps[:], lhs, rhs, start=True, stop=True).then_inc(stat_full, 1)

            proj(0, 0)
            proj(0, 1)
            pe.wait_ge(wlora_in, g * 16 + 16)
            stat("dec0", wlora[0:HEAD, :], z_t[0:HEAD, 0:HALF])
            proj(1, 0)
            stat("dec1", wlora[0:HEAD, :], z_t[0:HEAD, HALF:SEQ])
            stat("icl0", wlora[HEAD:P, :], z_t[HEAD:P, 0:HALF])
            proj(1, 1)
            stat("icl1", wlora[HEAD:P, :], z_t[HEAD:P, HALF:SEQ])
            pe.wait_ge(kk_squared, g + 1)
            stat("kk0", av64, sq[:, 0:HALF])
            proj(2, 0)
            stat("kk1", av64, sq[:, HALF:SEQ])
            proj(2, 1)
            proj(3, 0)
            proj(3, 1)

            def part(j, n):
                h, k = n // KT, n % KT
                if k == 0:
                    proj_begin(j, h)
                ins = project((j + 1) % 2, h, [k], proj_ps[:, h, :])
                if k == KT - 1:
                    ins.then_inc(proj_full, 1)

            def rk_begin(job):
                n = rk_no[job]
                pe.wait_ge(rk_free, g * NRK + (max(n - 1, 0) + FROM))
                settled(pe)
                return rk_ps[:, n % 2, :]

            def at_begin(job):
                n = at_no[job]
                if n == 0:
                    pe.wait_ge(turn_free, g * NTURN + NTURN)
                elif n >= 3:
                    pe.wait_ge(*at_freed(g, AT_JOBS[n - 3]))
                return at_ps[:, n % 3, :]

            def turn(n):
                a, h = TURNS[n]
                src = (v_b, kk_b, k_b)[a]
                if n == 0:
                    pe.wait_ge(at_free, g * NAD + FROM)
                elif n >= 3:
                    pe.wait_ge(turn_free, g * NTURN + (n - 2))
                settled(pe)
                for c in range(8):
                    for hd in range(2):
                        r = rows(hd)
                        t0 = (8 * h + c) * CH
                        ins = T.matmul(at_ps[r, n % 3, c * CH:(c + 1) * CH], src[r, t0:t0 + CH],
                                       cst[r, C_ID + hd * HEAD:C_ID + hd * HEAD + HEAD], start=True, stop=True)
                ins.then_inc(turn_full, 1)

            def chunk_products(name, q):
                src = kk_b if name == "ab" else k_b
                bank = rk_begin((name, q))
                for i in range(4):
                    c = 4 * q + i
                    for hd in range(2):
                        r = rows(hd)
                        ins = T.matmul(bank[r, i * P:(i + 1) * P], src[r, c * CH:(c + 1) * CH],
                                       ar_t[r, c, :, :].rearrange("p x t -> p (x t)"), start=True, stop=True)
                ins.then_inc(rk_full, 1)

            def turn_values(n):
                bank = at_begin(("v", n))
                for i in range(4):
                    t = 4 * n + i
                    ins = T.transpose(bank[:, i * P:(i + 1) * P], v_b[:, t * P:(t + 1) * P], ident)
                ins.then_inc(at_full, 1)

            MERGES = ((0, ab_m[:, :, 0, :], x_m), (1, xt_m, w_m), (2, w_m, xt_m), (3, ab_m[:, :, 0, :], x_m),
                      (4, w_m, xt_m))

            def merge(n):
                m, lhs, rhs = MERGES[n // 2]
                h = n % 2
                bank = rk_begin(("merge", m, h))
                for c in range(8):
                    for hd in range(2):
                        r = rows(hd)
                        ins = T.matmul(bank[r, c * CH:(c + 1) * CH], lhs[r, 8 * h + c, :], rhs[r, 8 * h + c, :],
                                       start=True, stop=True)
                ins.then_inc(rk_full, 1)

            for n in range(2 * KT):
                part(4, n)
                if n in (3, 5):
                    h = (n - 3) // 2
                    stat(f"q{h}", av64, q_sqs[:, cols(h)])
                if n == 6:
                    pe.wait_ge(tildes, g + 1)
                if 6 <= n < 10:
                    chunk_products("ab", n - 6)
                if n in (10, 12):
                    h = (n - 10) // 2
                    stat(f"rk{h}", av64, sq[:, cols(h)])
                if n in (11, 13, 15):
                    turn((n - 11) // 2)
            for n in range(2 * KT):
                part(5, n)
                if n < 3:
                    turn(n + 3)
                if n in (5, 7):
                    h = (n - 5) // 2
                    stat(f"k{h}", av64, k_sqs[:, cols(h)])
                if n >= 12:
                    chunk_products("ak", n - 12)
            for n in range(2 * KT):
                part(6, n)
                if n == 1:
                    pe.wait_ge(proj_free, g * NPJ + (4 + 2 * 5))
                    pe.wait_ge(qk_done, g * 2 + 1)
                if n in (1, 2):
                    turn_values(n - 1)
                if n == 4:
                    pe.wait_ge(xblk_in, g * 256 + 256)
                if 4 <= n < 14:
                    merge(n - 4)

            def pair(col, terms, bank=0):
                settled(pe)
                for hd in range(2):
                    r = rows(hd)
                    for i, (lhs, rhs) in enumerate(terms):
                        ins = T.matmul(rk_ps[r, bank, col:col + CH], lhs[r], rhs[r], start=(i == 0),
                                       stop=(i == len(terms) - 1))
                return ins

            def scores(qb, m):
                for c in range(qb // 4 + 1):
                    w = min(HALF, P * (qb + 1) - HALF * c)
                    bank = at_begin(("s", qb, m, c))
                    T.matmul(bank[:, 0:w], q_z[:, m, qb * P:(qb + 1) * P], kq_b[:, HALF * c:HALF * c + w],
                             start=True, stop=True).then_inc(at_full, 1)

            def turn_attn(qb):
                pe.wait_ge(attn_done, g * TT + (qb + 1))
                for c in range(qb // 4 + 1):
                    bank = at_begin(("t", qb, c))
                    for i in range(min(4, qb + 1 - 4 * c)):
                        ins = T.transpose(bank[:, i * P:(i + 1) * P], sc_b[:, 0, (4 * c + i) * P:(4 * c + i + 1) * P], ident)
                    ins.then_inc(at_full, 1)

            def weigh_values(qb):
                pe.wait_ge(*at_freed(g, ("t", qb, qb // 4)))
                bank = at_begin(("o", qb))
                for k in range(qb + 1):
                    ins = T.matmul(bank[:, 0:P], val[:, k, :], attn_t[:, k, :], start=(k == 0), stop=(k == qb))
                ins.then_inc(at_full, 1)

            GATE_AT = [c for c, n in enumerate(GATE_PARTS) for _ in range(n)]

            pe.wait_ge(rk_free, g * NRK + (NRK + FROM))
            pe.wait_ge(qk_done, g * 2 + 2)
            for c in range(NCH):
                qb, odd = c // 2, c % 2
                pe.wait_ge(s_done, g * (NCH + 1) + (c + 1))
                pair(0, [(ak_m[:, c, 0, :], v_t[:, c, :]), (ar_t[:, c, 0, :], s_t[:, c % 2, :])]).then_inc(step_full, 1)
                if not odd:
                    if qb >= 1:
                        turn_attn(qb - 1)
                    scores(qb, 0)
                for n in range(2 * KT):
                    if GATE_AT[n] == c:
                        part(7, n)
                pe.wait_ge(u0_done, g * NCH + (c + 1))
                pair(CH, [(xt_m[:, c, :], u0_t[:])]).then_inc(step_full, 1)
                if not odd:
                    scores(qb, 1)
                    if qb >= 1:
                        weigh_values(qb - 1)
                pe.wait_ge(u_done, g * NCH + (c + 1))
                pair(2 * CH, [(k_t[:, c, :], v_t[:, c, :]), (b_t[:, c, :], u_t[:, c % 2, :])]).then_inc(step_full, 1)
                if c % 8 == 0 and c > 0:
                    pe.wait_ge(y_out, g * 2 + c // 8)
                ins = pair((c % 8) * CH, [(s_t[:, c % 2, :], ar_t[:, c, 1, :]), (u_t[:, c % 2, :], ab_m[:, c, 1, :]),
                                          (v_t[:, c, :], ak_m[:, c, 1, :])], bank=1)
                if c % 8 == 7:
                    ins.then_inc(y_full, 1)
                if c == 8:
                    stat("ym0", av64, y_half[0])
                if c == 10:
                    pe.wait_ge(y_sq, g * 2 + 1)
                    stat("yv0", av64, y_sqs)
                if c == 13:
                    pe.wait_ge(o_sq, g * 2 + 1)
                    stat("om0", av128, o_sqs)
            turn_attn(TT - 1)
            pe.wait_ge(y_out, g * 2 + 2)
            stat("ym1", av64, y_half[1])
            weigh_values(TT - 1)
            pe.wait_ge(y_sq, g * 2 + 2)
            stat("yv1", av64, y_sqs)
            pe.wait_ge(o_sq, g * 2 + 2)
            stat("om1", av128, o_sqs)

        for s in range(4):
            for e in range(KT):
                if s == 0:
                    pe.wait_ge(m_split, e + 1)
                    pe.wait_ge(wo_split, e + 1)
                for i in range(4):
                    n = 4 * s + i
                    if e == 0 and s >= 2:
                        pe.wait_ge(out_sum, n - 7)
                    t = slice((n // 2) * P, (n // 2 + 1) * P)
                    ins = three(out_banks[n % 8], hn_hi[:, e, t], hn_lo[:, e, t], wo_hi[:, e, cols(n % 2)],
                                wo_lo[:, e, cols(n % 2)], e == 0, e == KT - 1)
                    if e == KT - 1:
                        ins.then_inc(out_full, 1)


def host_constants():
    p = np.arange(P)
    cst = np.zeros((P, C_WIDTH), np.float32)
    cst[:, C_ID:C_ID + P] = np.eye(P)
    cst[:, C_AV64:C_AV64 + P] = (p[:, None] // HEAD == p[None, :] // HEAD) / HEAD
    cst[:, C_AV128:C_AV128 + P] = 1.0 / P
    s, t = (p % CH)[:, None], np.arange(CH)[None, :]
    cst[:, C_AMASK:C_AMASK + CH] = s < t
    cst[:, C_AMASK + CH:C_AMASK + 2 * CH] = s <= t
    row, col = s, t
    cst[:, C_M1:C_M1 + CH] = ((row // 32) == (col // 32)) & ((row // 16) % 2 == 1) & ((col // 16) % 2 == 0)
    cst[:, C_M2:C_M2 + CH] = (row >= 32) & (col < 32)
    cst[:, C_EYE:C_EYE + BLK] = np.eye(SUB).reshape(1, BLK)
    dist = p[:, None] + (SEQ - P) - np.arange(SEQ)[None, :]
    slopes = [2.0 ** (-8.0 * (h + 1) / GROUPS) for h in range(GROUPS)]
    alibi = np.stack([np.where(dist >= 0, -sl * dist, -1e30) for sl in slopes]).astype(np.float32)
    return cst, alibi


def kernel(x, norm_g, w_in, shift_mu, w0, w_decay_up, a0, w_iclr_up, k_k, k_a, r_k, ln_x_w, ln_x_b,
           q_norm_g, k_norm_g, lambda_q1, lambda_k1, lambda_q2, lambda_k2, subln_g, w_out):
    import concourse.bacc as _bacc
    from concourse.bass_utils import run_bass_kernel_spmd as _run

    A = np.asarray
    W = GROUPS * P

    def tiles(w):
        w = A(w)
        return w.reshape(KT, P, w.shape[1] // P, P).transpose(2, 1, 0, 3).reshape(-1, P, SEQ)

    wt = tiles(A(w_in)[0])
    order = [12]
    for g in range(GROUPS):
        order += [4 + g, g, 8 + g, 17 + g, 21 + g, 25 + g, 13 + g, 29 + g]
    w_all = np.ascontiguousarray(np.concatenate([wt[order], A(w_out)[0].reshape(KT, P, D_MODEL)]))

    def per_group(v):
        return A(v).reshape(GROUPS, P).T

    mu = A(shift_mu)[0]
    prm = np.ascontiguousarray(np.stack([per_group(v) for v in (
        mu[0:W], mu[W:2 * W], mu[2 * W:3 * W], A(w0)[0], A(a0)[0], A(k_k)[0], A(k_a)[0], A(r_k)[0],
        A(ln_x_w)[0], A(ln_x_b)[0])], axis=2))
    qg, kg = A(q_norm_g)[0], A(k_norm_g)[0]
    shared = np.ascontiguousarray(np.stack([mu[3 * W:], np.tile(qg, 2), np.tile(kg, 2), A(subln_g)[0]], axis=1))
    lam_in = np.ascontiguousarray(np.broadcast_to(
        np.stack([A(lambda_q1)[0], A(lambda_q2)[0], A(lambda_k1)[0], A(lambda_k2)[0]])[None], (P, 4, HEAD)))
    ng = np.ascontiguousarray(A(norm_g)[0].reshape(KT, P).T)
    w_lora = np.concatenate([A(w_decay_up)[0], A(w_iclr_up)[0]]).reshape(P, GROUPS, P).transpose(1, 0, 2)
    w_lora = np.ascontiguousarray(np.concatenate([w_lora, w_lora[:1]]))
    cst, alibi = host_constants()
    arrays = {"x": np.ascontiguousarray(A(x)[0]), "w_all": w_all, "prm": prm, "shared": shared, "lam_in": lam_in,
              "norm_g": ng, "w_lora": w_lora, "consts": cst, "alibi": alibi}
    nc = _bacc.Bacc("TRN2", target_bir_lowering=False, num_devices=1)
    args = [nc.dram_tensor(n, a.shape, F32, kind="ExternalInput").ap() for n, a in arrays.items()]
    args.append(nc.dram_tensor("out", (SEQ, D_MODEL), F32, kind="ExternalOutput").ap())
    for n, s in (("mixed", (KT, P, SEQ)), ("nblk_d", (8, NCH, SUB, SUB)), ("xblk_d", (2, 8, NCH, SUB, SUB))):
        args.append(nc.dram_tensor(n, s, F32, kind="Internal").ap())
    with ExitStack() as ctx:
        build(nc, ctx, *args)
    r = _run(nc, [arrays], core_ids=[0])
    return r.results[0]["out"].reshape(1, SEQ, D_MODEL)
```

```python
from contextlib import ExitStack

import numpy as np
import concourse.bass as bass
from concourse import mybir

F32 = mybir.dt.float32
F32R = mybir.dt.float32r
ALU = mybir.AluOpType
ACT = mybir.ActivationFunctionType
AX_X = mybir.AxisListType.X

P = 128
SEQ = 1024
D_MODEL = 1024
KT = D_MODEL // P
TT = SEQ // P
HALF = 512
GROUPS = 4
HEAD = 64
CH = 64
NCH = SEQ // CH
SUB = 16
BLK = SUB * SUB
JOBS = 8
DECAY_MAX = float(np.exp(-0.5))
NORM_EPS = 1e-6
GN_EPS = 64e-5
SUBLN_EPS = 1e-5
LAMBDA_INIT = 0.8 - 0.6
PAD = 4

MU_R, MU_K, MU_V, W0, A0, K_K, K_A, R_K, LN_W, LN_B = range(10)
N_PRM = 10
OM_R, OM_K, OM_V, OM_KA, HALF_W0, HALF_A0 = range(10, 16)
N_DER = 16
MU_Z, Q_G, K_G, SUB_G, OM_Z, Q_GS, SUB_GS = range(7)
C_ID, C_AV64, C_AV128, C_AMASK, C_M1, C_M2, C_EYE = 0, 128, 256, 384, 512, 576, 640
C_WIDTH = 640 + BLK


def mix_order():
    return ([g for g in range(GROUPS - 1)] + [GROUPS + g for g in range(GROUPS - 1)]
            + [GROUPS - 1, 2 * GROUPS - 1])


def build(nc, ctx, x, w_all, prm, shared, lam_in, norm_g, w_lora, consts, alibi, out,
          mixed_dram, nblk_dram, xblk_dram):

    def sem(name):
        return ctx.enter_context(nc.semaphore(name))

    def sb(name, shape, dt=F32):
        return ctx.enter_context(nc.sbuf_tensor(name, shape, dt))

    proj_ps = ctx.enter_context(nc.psum_tensor("proj_ps", [P, 2, HALF], F32))
    stat_ps = ctx.enter_context(nc.psum_tensor("stat_ps", [P, HALF], F32))
    rk_ps = ctx.enter_context(nc.psum_tensor("rk_ps", [P, 2, HALF], F32))
    at_ps = ctx.enter_context(nc.psum_tensor("at_ps", [P, 3, HALF], F32))

    hn_hi = sb("hn_hi", [P, KT, SEQ], F32R)
    hn_lo = sb("hn_lo", [P, KT, SEQ], F32R)
    w_raw = sb("w_raw", [P, 2, SEQ])
    w_hi = sb("w_hi", [P, 2, SEQ], F32R)
    w_lo = sb("w_lo", [P, 2, SEQ], F32R)
    cst = sb("cst", [P, C_WIDTH])
    ident = cst[:, C_ID:C_ID + P]
    av64 = cst[:, C_AV64:C_AV64 + P]
    av128 = cst[:, C_AV128:C_AV128 + P]
    eps = sb("eps", [P, 4])
    zero_t = sb("zero_t", [P, CH])
    out_banks = [proj_ps[:, 0, :], proj_ps[:, 1, :], rk_ps[:, 1, :], at_ps[:, 0, :],
                 at_ps[:, 1, :], at_ps[:, 2, :], stat_ps[:], rk_ps[:, 0, :]]
    amask = cst[:, C_AMASK:C_AMASK + 2 * CH]
    m1mask = cst[:, C_M1:C_M1 + CH]
    m2mask = cst[:, C_M2:C_M2 + CH]

    loop_mem = ExitStack()

    def lb(name, shape, dt=F32):
        return loop_mem.enter_context(nc.sbuf_tensor(name, shape, dt))

    prm_all = lb("prm_all", [P, GROUPS + 1, N_DER])
    shr = lb("shr", [P, 8])
    ng = lb("ng", [P, KT])
    small = lb("small", [P, 32])
    cur = lb("cur", [P, N_DER])
    ln_wb = lb("ln_wb", [P, 2])
    wlora = lb("wlora", [P, P])
    z_t = lb("z_t", [P, SEQ])
    shift_raw = lb("shift_raw", [P, PAD + SEQ])
    bias_t = lb("bias_t", [P, SEQ])
    k_b = lb("k_b", [P, SEQ])
    r_b = lb("r_b", [P, SEQ])
    v_b = lb("v_b", [P, SEQ])
    kk_b = lb("kk_b", [P, SEQ])
    ar_t = lb("ar_t", [P, NCH, 2, CH])
    work = lb("work", [P, 7, SEQ])
    v_t = lb("v_t", [P, NCH, CH])
    b_t = lb("b_t", [P, NCH, CH])
    k_t = lb("k_t", [P, NCH, CH])
    s_t = lb("s_t", [P, 2, CH])
    sp_t = lb("sp_t", [P, CH])
    u0_t = lb("u0_t", [P, CH])
    u_t = lb("u_t", [P, 2, CH])
    pc = lb("pc", [P, NCH])
    q_z = lb("q_z", [P, 2, SEQ])
    kq_b = lb("kq_b", [P, SEQ])
    val = lb("val", [P, TT, P])
    sc_b = lb("sc_b", [P, 2, SEQ])
    attn_t = lb("attn_t", [P, TT, P])
    bonus = lb("bonus", [P, SEQ])
    o_b = lb("o_b", [P, SEQ])

    lw, cc, aa, e1, ex, sq, nrm = (work[:, i, :] for i in range(7))
    ab_m = work[:, 0:2, :].rearrange("p a (c x t) -> p (a c) x t", x=2, t=CH)
    ak_m = work[:, 2:4, :].rearrange("p a (c x t) -> p (a c) x t", x=2, t=CH)
    x_m = work[:, 4, :].rearrange("p (c t) -> p c t", t=CH)
    xt_m = work[:, 5, :].rearrange("p (c t) -> p c t", t=CH)
    w_m = work[:, 6, :].rearrange("p (c t) -> p c t", t=CH)
    nblk = work[:, 6, 0:BLK].rearrange("p (s t) -> p s t", t=SUB)
    xblk = work[:, 6, BLK:2 * BLK].rearrange("p (t s) -> p t s", s=SUB)
    xblkt = work[:, 6, 2 * BLK:3 * BLK].rearrange("p (s t) -> p s t", t=SUB)
    prod = work[:, 6, 3 * BLK:4 * BLK].rearrange("p (t s) -> p t s", s=SUB)
    x_in = [k_b, r_b, v_b, kk_b, bonus, ar_t[:, 0:8, :, :].rearrange("p c x t -> p (c x t)"), kq_b, o_b]
    ga_b, gb_b = r_b, kk_b
    mx, nm, ls, rl, c1 = small[:, 0:4], small[:, 4:6], small[:, 6:8], small[:, 8:10], small[:, 10:11]
    lam_neg = small[:, 11:12]
    ssq, rstd = small[:, 12:20], small[:, 20:28]
    lam_dot, lam_e = small[:, 28:30], small[:, 30:32]
    lam_sb = work[:, 2, 0:4 * HEAD].rearrange("p (a b) -> p a b", b=HEAD)
    x_scr = [work[:, 0, :], work[:, 1, :]]
    y_half = [k_b[:, 0:HALF], kq_b[:, 0:HALF]]
    y_sqs, y_nrm = v_b[:, 0:HALF], v_b[:, HALF:SEQ]
    o_sqs, o_nrm = work[:, 6, 0:HALF], work[:, 6, HALF:SEQ]
    ga_th, gb_th = o_b, shift_raw[:, PAD:PAD + SEQ]
    q_raw = o_b
    q_sqs, k_sqs = sc_b[:, 0, :], sc_b[:, 1, :]
    q_nrm, k_nrm = val.rearrange("p a b -> p (a b)"), attn_t.rearrange("p a b -> p (a b)")


    loop_mem.close()
    wo_hi = sb("wo_hi", [P, KT, SEQ], F32R)
    wo_lo = sb("wo_lo", [P, KT, SEQ], F32R)
    x_res = sb("x_res", [P, 2, SEQ])
    o_stage = sb("o_stage", [P, 2, SEQ])
    MIX = mix_order()
    EARLY = 2 * GROUPS - 2
    mixed_raw = [w_raw[:, 1, :], z_t[:], work[:, 4, :], w_raw[:, 1, :], o_stage[:, 0, :], x_res[:, 0, :], bonus[:], o_b[:]]
    w_out_raw = [None, w_raw[:, 0, :], w_raw[:, 0, :], z_t[:], o_stage[:, 1, :], x_res[:, 1, :], w_raw[:, 0, :], w_raw[:, 1, :]]
    ON_POOL = [("w", 1), ("m", 0), ("m", 1)]
    TAIL = [("m", 2), ("w", 2), ("m", 3), ("w", 3), ("m", 4), ("w", 4), ("m", 5), ("w", 5), ("m", 6), ("w", 6),
            ("m", 7), ("w", 7)]
    tail_no = {j: n for n, j in enumerate(TAIL)}

    def split_parts(job):
        kind, i = job
        if kind == "m":
            return mixed_raw[i], hn_hi[:, i, :], hn_lo[:, i, :]
        if i == 1:
            return w_out_raw[1], w_hi[:, 0, :], w_lo[:, 0, :]
        return w_out_raw[i], wo_hi[:, i, :], wo_lo[:, i, :]

    def load_tile(queue, job):
        kind, i = job
        if kind == "m":
            queue.dma_start(mixed_raw[i], mixed_dram[MIX[i]]).then_inc(m_in[i], 16)
        else:
            queue.dma_start(w_out_raw[i], w_all[GROUPS * JOBS + 1 + i]).then_inc(wo_in[i], 16)

    c_loaded = sem("c_loaded")
    x_loaded = [sem(f"x_loaded{t}") for t in range(TT)]
    w_loaded = [sem("w_loaded0"), sem("w_loaded1")]
    w_hi_done, w_split = sem("w_hi_done"), sem("w_split")
    proj_full, proj_free = sem("proj_full"), sem("proj_free")
    ssq_done, xn_done = sem("ssq_done"), sem("xn_done")
    turned, hi_done, hn_done = sem("turned"), sem("hi_done"), sem("hn_done")
    prm_done, lam_exp, z_shifted, z_done = sem("prm_done"), sem("lam_exp"), sem("z_shifted"), sem("z_done")
    group_set, wlora_in = sem("group_set"), sem("wlora_in")
    shifted = sem("shifted")
    stat_full, stat_free = sem("stat_full"), sem("stat_free")
    kk_squared, rk_in = sem("kk_squared"), sem("rk_in")
    scanned, exps_done = sem("scanned"), sem("exps_done")
    tildes = sem("tildes")
    turn_full, turn_free = sem("turn_full"), sem("turn_free")
    qk_scaled = sem("qk_scaled")
    qk_done = sem("qk_done")
    rk_full, rk_free = sem("rk_full"), sem("rk_free")
    nblk_out, nblk_in = sem("nblk_out"), sem("nblk_in")
    blocks_done, xblk_out, xblk_in = sem("blocks_done"), sem("xblk_out"), sem("xblk_in")
    x_zeroed = sem("x_zeroed")
    step_full = sem("step_full")
    u0_done, u_done, s_done = sem("u0_done"), sem("u_done"), sem("s_done")
    y_full, y_out = sem("y_full"), sem("y_out")
    y_sq, y_fin = sem("y_sq"), sem("y_fin")
    at_full, at_free = sem("at_full"), sem("at_free")
    weights_out = sem("weights_out")
    neg_done, exp_done, attn_done = sem("neg_done"), sem("exp_done"), sem("attn_done")
    o_sq, o_fin = sem("o_sq"), sem("o_fin")
    y_scaled, o_scaled = sem("y_scaled"), sem("o_scaled")
    bias_in, mixed_out = sem("bias_in"), sem("mixed_out")
    m_in = [sem(f"m_in{i}") for i in range(2 * GROUPS - 2)]
    wo_in = {i: sem(f"wo_in{i}") for i in range(2, KT)}
    pool_split = sem("pool_split")
    tail_hi, tail_split = sem("tail_hi"), sem("tail_split")
    res_in = [sem("res_in0"), sem("res_in1")]
    out_full, out_sum = sem("out_full"), sem("out_sum")
    stored = [sem("stored0"), sem("stored1")]

    FROM = 1
    from_one = [stat_free, rk_free, at_free, y_fin, o_fin, mixed_out]
    STATS = ["dec0", "dec1", "icl0", "icl1", "kk0", "kk1", "q0", "q1", "rk0", "rk1", "k0", "k1",
             "ym0", "yv0", "om0", "ym1", "yv1", "om1"]
    NST = len(STATS)
    stat_no = {s: n for n, s in enumerate(STATS)}
    step_bank = rk_ps[:, 0, :]

    def stat_bank(name):
        return step_bank if name == "om1" else stat_ps

    TURNS = [(a, h) for a in range(3) for h in range(2)]
    NTURN = len(TURNS)
    RK_JOBS = ([("ab", q) for q in range(4)] + [("ak", q) for q in range(4)]
               + [("merge", m, h) for m in range(5) for h in range(2)])
    NRK = len(RK_JOBS)
    rk_no = {j: n for n, j in enumerate(RK_JOBS)}
    AT_JOBS = [("v", 0), ("v", 1)]
    for qb in range(TT):
        nh = qb // 4 + 1
        if qb >= 1:
            AT_JOBS += [("t", qb - 1, c) for c in range((qb - 1) // 4 + 1)]
        AT_JOBS += [("s", qb, m, c) for m in range(2) for c in range(nh)]
        if qb >= 1:
            AT_JOBS += [("o", qb - 1)]
    AT_JOBS += [("t", TT - 1, c) for c in range(2)] + [("o", TT - 1)]
    NAT = len(AT_JOBS)
    at_no = {j: n for n, j in enumerate(AT_JOBS)}
    on_act = [j for j in AT_JOBS if j[0] == "t"]
    on_dve = [j for j in AT_JOBS if j[0] != "t"]
    NTA, NAD = len(on_act), len(on_dve)

    def at_freed(g, job):
        if job[0] == "t":
            return weights_out, g * NTA + (on_act.index(job) + 1)
        return at_free, g * NAD + (on_dve.index(job) + 1 + FROM)
    NPJ = 2 * JOBS
    NSTEP = 3 * NCH

    GATE_PARTS = [1, 2, 1, 2, 0, 2, 0, 2, 0, 2, 0, 2, 0, 2]

    def cols(h):
        return slice(h * HALF, (h + 1) * HALF)

    def rows(h):
        return slice(h * HEAD, (h + 1) * HEAD)

    passed = {e.engine: sem(f"passed{i}") for i, e in enumerate((nc.tensor, nc.vector, nc.gpsimd, nc.sync))}

    def settled(eng):
        eng.sem_inc(passed[eng.engine], 1)

    block = ctx.enter_context(nc.Block())

    @block.sync
    def _(sp):
        for s in from_one:
            sp.sem_inc(s, FROM)
        def load_x(t):
            sp.dma_start(x_in[t][:], x[t * P:(t + 1) * P, :]).then_inc(x_loaded[t], 16)

        for t in range(TT // 2):
            load_x(t)
        sp.dma_start(cst[:], consts).then_inc(c_loaded, 16)
        sp.dma_start(prm_all[:, 0:GROUPS, 0:N_PRM], prm).then_inc(c_loaded, 16)
        sp.dma_start(shr[:, 0:4], shared).then_inc(c_loaded, 16)
        sp.dma_start(ng[:], norm_g).then_inc(c_loaded, 16)
        sp.dma_start(lam_sb, lam_in).then_inc(c_loaded, 16)
        sp.dma_start(wlora[:], w_lora[0]).then_inc(wlora_in, 16)
        sp.dma_start(w_raw[:, 0, :], w_all[0]).then_inc(w_loaded[0], 16)
        for t in range(TT // 2, TT):
            load_x(t)
        sp.dma_start(w_raw[:, 1, :], w_all[1]).then_inc(w_loaded[1], 16)
        sp.wait_ge(w_split, 1)
        sp.dma_start(w_raw[:, 0, :], w_all[2]).then_inc(w_loaded[0], 16)
        with sp.Fori(0, GROUPS) as g:
            sp.wait_ge(at_free, g * NAD + FROM)
            settled(sp)
            sp.dma_start(bias_t[:], alibi[bass.ds(g, 1)].rearrange("o p c -> (o p) c")).then_inc(bias_in, 16)
            for j in range(JOBS):
                sp.wait_ge(w_split, g * JOBS + (j + 2))
                sp.dma_start(w_raw[:, (j + 1) % 2, :],
                             w_all[bass.ds(g * JOBS + (j + 3), 1)].rearrange("o p c -> (o p) c")
                             ).then_inc(w_loaded[(j + 1) % 2], 16)
                if j == 2:
                    sp.wait_ge(stat_free, g * NST + (stat_no["icl1"] + 1 + FROM))
                    sp.dma_start(wlora[:], w_lora[bass.ds(g + 1, 1)].rearrange("o p n -> (o p) n")).then_inc(wlora_in, 16)
                if j == 4:
                    sp.wait_ge(rk_free, g * NRK + (rk_no["ab", 3] + 1 + FROM))
                    for i in range(8):
                        sp.dma_start(nblk_dram[i].rearrange("c s t -> s c t"),
                                     ab_m[SUB * i:SUB * i + SUB, :, 0, SUB * (i % 4):SUB * (i % 4) + SUB]
                                     ).then_inc(nblk_out, 16)
                    sp.wait_ge(nblk_out, g * 128 + 128)
                    settled(sp)
                    sp.wait_ge(tildes, g + 1)
                    sp.dma_start(nblk, nblk_dram.rearrange("i c s t -> (i c) s t")).then_inc(nblk_in, 16)
                if j == 5:
                    sp.wait_ge(blocks_done, g + 1)
                    sp.dma_start(xblk_dram[0].rearrange("i c t s -> (i c) t s"), xblk).then_inc(xblk_out, 16)
                    sp.dma_start(xblk_dram[1].rearrange("i c t s -> (i c) t s"), xblkt).then_inc(xblk_out, 16)
                    sp.wait_ge(xblk_out, g * 32 + 32)
                    sp.wait_ge(x_zeroed, g + 1)
                    for n, dst in ((0, x_m), (1, xt_m)):
                        for i in range(8):
                            sp.dma_start(dst[SUB * i:SUB * i + SUB, :, SUB * (i % 4):SUB * (i % 4) + SUB],
                                         xblk_dram[n, i].rearrange("c t s -> t c s")).then_inc(xblk_in, 16)
            sp.wait_ge(o_fin, g * 2 + (2 + FROM))
            sp.dma_start(mixed_dram[bass.ds(g + GROUPS, 1)].rearrange("o p c -> (o p) c"), o_b[:]).then_inc(mixed_out, 16)
            sp.wait_ge(y_fin, g * 2 + (2 + FROM))
            sp.dma_start(mixed_dram[bass.ds(g, 1)].rearrange("o p c -> (o p) c"), bonus[:]).then_inc(mixed_out, 16)
        sp.wait_ge(wlora_in, 16 * (GROUPS + 1))
        for job in (("m", 4), ("w", 4), ("m", 5), ("w", 5)):
            load_tile(sp, job)
        for job, before in ((("w", 6), ("w", 2)), (("w", 7), ("m", 3))):
            sp.wait_ge(tail_split, tail_no[before] + 1)
            load_tile(sp, job)
        sp.wait_ge(tail_split, tail_no["w", 5] + 1)
        for t in range(TT):
            if t >= 2:
                sp.wait_ge(out_sum, 2 * t - 2)
            sp.dma_start(x_res[:, t % 2, :], x[t * P:(t + 1) * P, :]).then_inc(res_in[t % 2], 16)
            if t >= 1:
                sp.wait_ge(out_sum, 2 * t)
                sp.dma_start(out[(t - 1) * P:t * P, :], o_stage[:, (t - 1) % 2, :]).then_inc(stored[(t - 1) % 2], 16)
        sp.wait_ge(out_sum, 2 * TT)
        sp.dma_start(out[(TT - 1) * P:TT * P, :], o_stage[:, (TT - 1) % 2, :]).then_inc(stored[(TT - 1) % 2], 16)
        for s in stored:
            sp.wait_ge(s, 16 * TT // 2)
        sp.wait_ge(mixed_out, 32 * GROUPS + FROM)

    @block.gpsimd
    def _(pool):
        for n in range(2):
            pool.wait_ge(w_hi_done, n + 1)
            nc.gpsimd.tensor_tensor(w_lo[:, n, :], w_raw[:, n, :], w_hi[:, n, :].bitcast(F32),
                                    ALU.subtract).then_inc(w_split, 1)
        with pool.Fori(0, GROUPS) as g:
            for j in range(JOBS):
                if j == 5:
                    pool.wait_ge(stat_free, g * NST + (stat_no["rk1"] + 1 + FROM))
                    settled(pool)
                    nc.gpsimd.memset(work[:, 4:6, :], 0.0).then_inc(x_zeroed, 1)
                pool.wait_ge(w_hi_done, g * JOBS + (j + 3))
                nc.gpsimd.tensor_tensor(w_lo[:, j % 2, :], w_raw[:, j % 2, :], w_hi[:, j % 2, :].bitcast(F32),
                                        ALU.subtract).then_inc(w_split, 1)
        pool.wait_ge(proj_full, GROUPS * NPJ + 2)
        pool.wait_ge(w_split, GROUPS * JOBS + 2)
        pool.wait_ge(mixed_out, 32 * (GROUPS - 1) + FROM)
        load_tile(nc.gpsimd, ("m", 0))
        load_tile(nc.gpsimd, ("m", 1))
        load_tile(nc.gpsimd, ("m", 2))
        for n, job in enumerate(ON_POOL):
            raw, high_part, low_part = split_parts(job)
            if job[0] == "m":
                pool.wait_ge(m_in[job[1]], 16)
            else:
                pool.wait_ge(w_loaded[0], 16 * ((GROUPS * JOBS + 2) // 2 + 1))
            nc.gpsimd.tensor_copy(high_part, raw)
            pool.drain()
            nc.gpsimd.tensor_tensor(low_part, raw, high_part.bitcast(F32), ALU.subtract).then_inc(pool_split, 1)
            pool.wait_ge(pool_split, n + 1)
            load_tile(nc.gpsimd, (("w", 2), ("m", 3), ("w", 3))[n])

    @block.scalar
    def _(act):
        def high(n):
            act.wait_ge(turned, n + 1)
            nc.scalar.activation(hn_hi[:, n % KT, cols(n // KT)], at_ps[:, n % 3, :], ACT.Copy,
                                 scale=ng[:, n % KT:n % KT + 1]).then_inc(hi_done, 1)

        def root_means(h):
            for t in range(4 * h, 4 * h + 4):
                act.wait_ge(x_loaded[t], 16)
                if t >= 2:
                    act.drain()
                nc.scalar.activation(x_scr[t % 2], x_in[t][:], ACT.Square, accum_out=ssq[:, t:t + 1])
            act.drain()
            act.wait_ge(prm_done, 1)
            nc.scalar.activation(rstd[:, 4 * h:4 * h + 4], ssq[:, 4 * h:4 * h + 4], ACT.Sqrt, scale=1.0 / D_MODEL,
                                 bias=eps[:, 0:1]).then_inc(ssq_done, 1)

        def weights_high(n):
            act.wait_ge(w_loaded[n], 16)
            nc.scalar.activation(w_hi[:, n, :], w_raw[:, n, :], ACT.Copy).then_inc(w_hi_done, 1)

        root_means(0)
        weights_high(0)
        for n in range(KT):
            high(n)
        root_means(1)
        nc.scalar.activation(lam_e, lam_dot, ACT.Exp).then_inc(lam_exp, 1)
        weights_high(1)
        for n in range(KT, 2 * KT):
            high(n)
        for h in range(2):
            act.wait_ge(proj_full, h + 1)
            nc.scalar.activation(shift_raw[:, PAD + h * HALF:PAD + (h + 1) * HALF], proj_ps[:, h, :], ACT.Copy)
            nc.scalar.activation(z_t[:, cols(h)], proj_ps[:, h, :], ACT.Copy,
                                 scale=shr[:, OM_Z:OM_Z + 1]).then_inc(proj_free, 1)
        act.wait_ge(z_shifted, 1)
        nc.scalar.activation(z_t[0:HEAD, :], z_t[0:HEAD, :], ACT.Tanh).then_inc(z_done, 1)

        with act.Fori(0, GROUPS) as g:
            def next_hi(j):
                act.wait_ge(w_loaded[j % 2], g * 64 + 16 * (j // 2 + 2))
                act.wait_ge(proj_full, g * NPJ + (2 + 2 * j))
                nc.scalar.activation(w_hi[:, j % 2, :], w_raw[:, j % 2, :], ACT.Copy).then_inc(w_hi_done, 1)

            def take_shifted(j, h, dst, om):
                act.wait_ge(proj_full, g * NPJ + (3 + 2 * j + h))
                nc.scalar.activation(shift_raw[:, PAD + h * HALF:PAD + (h + 1) * HALF], proj_ps[:, h, :], ACT.Copy)
                nc.scalar.activation(dst[:, cols(h)], proj_ps[:, h, :], ACT.Copy,
                                     scale=cur[:, om:om + 1]).then_inc(proj_free, 1)

            def take_two(j, h, dst, dst2, func, scale):
                act.wait_ge(proj_full, g * NPJ + (3 + 2 * j + h))
                nc.scalar.activation(dst[:, cols(h)], proj_ps[:, h, :], ACT.Copy)
                nc.scalar.activation(dst2[:, cols(h)], proj_ps[:, h, :], func, scale=scale).then_inc(proj_free, 1)

            def stat_to(name, dst, func, scale=1.0, bias=0.0):
                act.wait_ge(stat_full, g * NST + (stat_no[name] + 1))
                nc.scalar.activation(dst, stat_bank(name)[:], func, scale=scale, bias=bias).then_inc(stat_free, 1)

            half_w0, half_a0 = cur[:, HALF_W0:HALF_W0 + 1], cur[:, HALF_A0:HALF_A0 + 1]
            next_hi(0)
            act.wait_ge(group_set, g + 1)
            take_shifted(0, 0, k_b, OM_K)
            take_shifted(0, 1, k_b, OM_K)
            stat_to("dec0", lw[:, 0:HALF], ACT.Tanh, 0.5, half_w0)
            stat_to("dec1", lw[:, HALF:SEQ], ACT.Tanh, 0.5, half_w0)
            stat_to("icl0", aa[:, 0:HALF], ACT.Tanh, 0.5, half_a0)
            stat_to("icl1", aa[:, HALF:SEQ], ACT.Tanh, 0.5, half_a0)
            next_hi(1)
            act.wait_ge(shifted, g * 3 + 1)
            nc.scalar.activation(sq, k_b[:], ACT.Square, scale=cur[:, K_K:K_K + 1]).then_inc(kk_squared, 1)
            act.wait_ge(o_fin, g * 2 + FROM)
            act.wait_ge(y_fin, g * 2 + FROM)
            take_shifted(1, 0, r_b, OM_R)
            stat_to("kk0", nrm[:, 0:HALF], ACT.Sqrt, float(HEAD))
            stat_to("kk1", nrm[:, HALF:SEQ], ACT.Sqrt, float(HEAD))
            take_shifted(1, 1, r_b, OM_R)
            next_hi(2)
            act.wait_ge(scanned, g + 1)
            nc.scalar.activation(e1, cc, ACT.Exp)
            nc.scalar.activation(ex, ex, ACT.Exp)
            act.drain()
            nc.scalar.activation(cc, cc, ACT.Exp, scale=-1.0).then_inc(exps_done, 1)
            act.wait_ge(shifted, g * 3 + 2)
            take_shifted(2, 0, v_b, OM_V)
            take_shifted(2, 1, v_b, OM_V)
            next_hi(3)
            act.wait_ge(mixed_out, g * 32 + FROM)
            for h in range(2):
                take_two(3, h, q_raw, q_sqs, ACT.Square, 1.0)
            next_hi(4)
            for h in range(2):
                stat_to(f"q{h}", q_nrm[:, cols(h)], ACT.Ln, 1.0, eps[:, 0:1])
            act.drain()
            nc.scalar.activation(q_nrm, q_nrm, ACT.Exp, scale=-0.5).then_inc(qk_scaled, 1)
            take_two(4, 0, kq_b, k_sqs, ACT.Square, 1.0)

            def turned_out(n):
                a, h = TURNS[n]
                act.wait_ge(turn_full, g * NTURN + (n + 1))
                nc.scalar.activation((v_t, b_t, k_t)[a][:, 8 * h:8 * h + 8, :],
                                     at_ps[:, n % 3, :].rearrange("p (c d) -> p c d", d=CH), ACT.Copy
                                     ).then_inc(turn_free, 1)

            def value_out(h):
                act.wait_ge(proj_full, g * NPJ + (3 + 2 * 5 + h))
                nc.scalar.activation(v_b[:, cols(h)], proj_ps[:, h, :], ACT.Copy).then_inc(proj_free, 1)

            for n in range(3):
                turned_out(n)
            take_two(4, 1, kq_b, k_sqs, ACT.Square, 1.0)
            next_hi(5)
            turned_out(3)
            turned_out(4)
            turned_out(5)
            act.wait_ge(stat_free, g * NST + (stat_no["rk1"] + 1 + FROM))
            for h in range(2):
                stat_to(f"k{h}", k_nrm[:, cols(h)], ACT.Ln, 1.0, eps[:, 0:1])
                value_out(h)
            act.drain()
            nc.scalar.activation(k_nrm, k_nrm, ACT.Exp, scale=-0.5).then_inc(qk_scaled, 1)
            next_hi(6)
            act.wait_ge(qk_done, g * 2 + 1)
            for h in range(2):
                take_two(6, h, r_b, ga_th, ACT.Tanh, 0.5)
            next_hi(7)

            def y_square(h):
                act.wait_ge(stat_free, g * NST + (stat_no[f"ym{h}"] + 1 + FROM))
                nc.scalar.activation(y_sqs, y_half[h], ACT.Square).then_inc(y_sq, 1)

            def o_square(h):
                act.wait_ge(*at_freed(g, ("o", 4 * h + 3)))
                nc.scalar.activation(o_sqs, o_b[:, cols(h)], ACT.Square).then_inc(o_sq, 1)

            def y_log(h):
                act.wait_ge(y_fin, g * 2 + (h + FROM))
                stat_to(f"yv{h}", y_nrm, ACT.Ln, 1.0, eps[:, 1:2])

            def inverse_roots(h):
                act.wait_ge(o_fin, g * 2 + (h + FROM))
                stat_to(f"om{h}", o_nrm, ACT.Ln, 1.0, eps[:, 2:3])
                act.drain()
                nc.scalar.activation(y_nrm, y_nrm, ACT.Exp, scale=-0.5).then_inc(y_scaled, 1)
                nc.scalar.activation(o_nrm, o_nrm, ACT.Exp, scale=-0.5).then_inc(o_scaled, 1)

            def weights_turned(qb):
                for c in range(qb // 4 + 1):
                    n = at_no["t", qb, c]
                    w = min(4, qb + 1 - 4 * c)
                    act.wait_ge(at_full, g * NAT + (n + 1))
                    nc.scalar.activation(attn_t[:, 4 * c:4 * c + w, :],
                                         at_ps[:, n % 3, 0:w * P].rearrange("p (a d) -> p a d", d=P), ACT.Copy
                                         ).then_inc(weights_out, 1)

            for c in range(0, NCH, 2):
                qb = c // 2
                if qb >= 1:
                    weights_turned(qb - 1)
                act.wait_ge(neg_done, g * TT + (qb + 1))
                for m in range(2):
                    ins = nc.scalar.activation(sc_b[:, m, 0:P * (qb + 1)], sc_b[:, m, 0:P * (qb + 1)], ACT.Exp,
                                               bias=nm[:, m:m + 1], accum_out=ls[:, m:m + 1])
                ins.then_inc(exp_done, 1)
                if c == 8:
                    take_two(7, 0, gb_b, gb_th, ACT.Tanh, 0.5)
                    y_square(0)
                if c == 14:
                    take_two(7, 1, gb_b, gb_th, ACT.Tanh, 0.5)
                if c == 10:
                    o_square(0)
                if c == 12:
                    y_log(0)
                if c == 14:
                    inverse_roots(0)
            weights_turned(TT - 1)
            y_square(1)
            o_square(1)
            y_log(1)
            inverse_roots(1)

        act.wait_ge(y_fin, 2 * GROUPS + FROM)
        act.wait_ge(o_fin, 2 * GROUPS + FROM)
        for job in TAIL:
            raw, high_part, _ = split_parts(job)
            if job[0] == "w":
                act.wait_ge(wo_in[job[1]], 16)
            elif job[1] < EARLY:
                act.wait_ge(m_in[job[1]], 16)
            nc.scalar.activation(high_part, raw, ACT.Copy).then_inc(tail_hi, 1)

    @block.vector
    def _(dve):
        V = nc.vector

        def affine(dst, src, a, b):
            return V.tensor_scalar(dst, src, a, b, ALU.mult, ALU.add)

        V.memset(shift_raw[:, 0:PAD], 0.0)
        V.memset(zero_t[:], 0.0)
        V.memset(eps[:, 0:1], NORM_EPS)
        V.memset(eps[:, 1:2], GN_EPS)
        V.memset(eps[:, 2:3], SUBLN_EPS)
        V.memset(prm_all[:, GROUPS, :], 0.0)
        V.memset(q_z[rows(1), 0, :], 0.0)
        V.memset(q_z[rows(0), 1, :], 0.0)
        dve.wait_ge(c_loaded, 16 * 5)
        affine(prm_all[:, 0:GROUPS, OM_R:OM_V + 1], prm_all[:, 0:GROUPS, MU_R:MU_V + 1], -1.0, 1.0)
        affine(prm_all[:, 0:GROUPS, OM_KA:OM_KA + 1], prm_all[:, 0:GROUPS, K_A:K_A + 1], -1.0, 1.0)
        V.tensor_scalar(prm_all[:, 0:GROUPS, HALF_W0:HALF_A0 + 1], prm_all[:, 0:GROUPS, W0:A0 + 1], 0.5, None, ALU.mult)
        affine(shr[:, OM_Z:OM_Z + 1], shr[:, MU_Z:MU_Z + 1], -1.0, 1.0)
        V.tensor_scalar(shr[:, Q_GS:Q_GS + 1], shr[:, Q_G:Q_G + 1], HEAD ** -0.5, None, ALU.mult)
        V.tensor_scalar(shr[:, SUB_GS:SUB_GS + 1], shr[:, SUB_G:SUB_G + 1], 1.0 - LAMBDA_INIT, None, ALU.mult)
        V.tensor_tensor(lam_sb[:, 0:2, :], lam_sb[:, 0:2, :], lam_sb[:, 2:4, :], ALU.mult)
        dve.drain()
        V.tensor_reduce(lam_dot, lam_sb[:, 0:2, :], AX_X, ALU.add).then_inc(prm_done, 1)
        def normalise(h):
            dve.wait_ge(ssq_done, h + 1)
            V.reciprocal(rstd[:, 4 * h:4 * h + 4], rstd[:, 4 * h:4 * h + 4])
            dve.drain()
            for t in range(4 * h, 4 * h + 4):
                V.tensor_scalar(x_in[t][:], x_in[t][:], rstd[:, t:t + 1], None, ALU.mult).then_inc(xn_done, 1)

        def low(n):
            dve.wait_ge(hi_done, n + 1)
            V.scalar_tensor_tensor(out=hn_lo[:, n % KT, cols(n // KT)], in0=at_ps[:, n % 3, :],
                                   scalar=ng[:, n % KT:n % KT + 1], in1=hn_hi[:, n % KT, cols(n // KT)].bitcast(F32),
                                   op0=ALU.mult, op1=ALU.subtract).then_inc(hn_done, 1)

        normalise(0)
        for n in range(KT):
            low(n)
        normalise(1)
        dve.wait_ge(lam_exp, 1)
        V.tensor_scalar(lam_neg, lam_e[:, 1:2], lam_e[:, 0:1], -LAMBDA_INIT, ALU.subtract, ALU.add)
        for n in range(KT, 2 * KT):
            low(n)
        dve.wait_ge(proj_free, 2)
        V.scalar_tensor_tensor(out=z_t[:], in0=shift_raw[:, PAD - 1:PAD - 1 + SEQ], scalar=shr[:, MU_Z:MU_Z + 1],
                               in1=z_t[:], op0=ALU.mult, op1=ALU.add).then_inc(z_shifted, 1)

        V.tensor_copy(cur[:], prm_all[:, 0, :])
        dve.drain().then_inc(group_set, 1)

        with dve.Fori(0, GROUPS) as g:
            def prm1(i):
                return cur[:, i:i + 1]

            def stt(dst, a, s, b, op0=ALU.mult, op1=ALU.mult):
                return V.scalar_tensor_tensor(out=dst, in0=a, scalar=s, in1=b, op0=op0, op1=op1)

            def mul(dst, a, b):
                return V.tensor_tensor(dst, a, b, ALU.mult)

            def shift(j, dst, mu):
                dve.wait_ge(proj_free, g * NPJ + (4 + 2 * j))
                stt(dst[:], shift_raw[:, PAD - 1:PAD - 1 + SEQ], prm1(mu), dst[:], ALU.mult, ALU.add).then_inc(shifted, 1)

            def rk_take(job):
                n = rk_no[job]
                dve.wait_ge(rk_full, g * NRK + (n + 1))
                return rk_ps[:, n % 2, :]

            def at_take(job):
                n = at_no[job]
                dve.wait_ge(at_full, g * NAT + (n + 1))
                return at_ps[:, n % 3, :]

            def sigmoid(buf):
                return affine(buf, buf, 0.5, 0.5)

            V.tensor_copy(ln_wb[:], cur[:, LN_W:LN_B + 1])
            shift(0, k_b, MU_K)
            dve.wait_ge(stat_free, g * NST + (2 + FROM))
            affine(lw, lw, -0.5 * DECAY_MAX, -0.5 * DECAY_MAX)
            dve.drain()
            for c in range(NCH):
                s = slice(c * CH, (c + 1) * CH)
                V.tensor_tensor_scan(cc[:, s], lw[:, s], zero_t[:], 0.0, ALU.add, ALU.add)
            dve.drain()
            V.tensor_tensor(ex, cc, lw, ALU.subtract).then_inc(scanned, 1)
            dve.wait_ge(stat_free, g * NST + (4 + FROM))
            sigmoid(aa)
            shift(1, r_b, MU_R)
            dve.drain()
            V.tensor_scalar(lw, aa, prm1(K_A), prm1(OM_KA), ALU.mult, ALU.add)
            for h in range(2):
                dve.wait_ge(stat_free, g * NST + (stat_no[f"kk{h}"] + 1 + FROM))
                V.tensor_scalar(nrm[:, cols(h)], nrm[:, cols(h)], 1e-12, None, ALU.max)
                dve.drain()
                V.reciprocal(nrm[:, cols(h)], nrm[:, cols(h)])
            dve.drain()
            stt(kk_b[:], k_b[:], prm1(K_K), nrm)
            dve.drain()
            mul(k_b[:], k_b[:], lw)
            shift(2, v_b, MU_V)
            dve.drain()
            stt(sq, r_b[:], prm1(R_K), k_b[:]).then_inc(rk_in, 1)
            dve.wait_ge(exps_done, g + 1)
            V.tensor_copy(pc[:], e1.rearrange("p (c t) -> p c t", t=CH)[:, :, CH - 1])
            ch3 = lambda ap: ap.rearrange("p (c t) -> p c t", t=CH)
            mul(ar_t[:, :, 1, :], ch3(r_b[:]), ch3(e1))
            stt(ar_t[:, :, 0, :], ch3(kk_b[:]), -1.0, ch3(ex))
            dve.drain()
            mul(kk_b[:], kk_b[:], aa)
            mul(k_b[:], k_b[:], cc)
            dve.drain()
            mul(kk_b[:], kk_b[:], cc).then_inc(tildes, 1)
            def chunk_matrices(name, dst):
                for q in range(4):
                    V.tensor_tensor(dst[:, 4 * q:4 * q + 4, :, :].rearrange("p c x t -> p c (x t)"),
                                    rk_take((name, q)).rearrange("p (c t) -> p c t", c=4),
                                    amask.unsqueeze(1).broadcast_to([P, 4, 2 * CH]), ALU.mult).then_inc(rk_free, 1)

            def qk_norm(n):
                dve.wait_ge(qk_scaled, g * 2 + (n + 1))
                if n == 0:
                    for m in range(2):
                        ins = stt(q_z[rows(m), m, :], q_raw[rows(m), :], shr[rows(m), Q_GS:Q_GS + 1], q_nrm[rows(m), :])
                else:
                    ins = stt(kq_b[:], kq_b[:], shr[:, K_G:K_G + 1], k_nrm)
                ins.then_inc(qk_done, 1)

            chunk_matrices("ab", ab_m)
            dve.wait_ge(mixed_out, g * 32 + FROM)
            for h in range(2):
                dve.wait_ge(stat_full, g * NST + (stat_no[f"rk{h}"] + 1))
                stt(bonus[:, cols(h)], stat_ps[:], float(HEAD), v_b[:, cols(h)]).then_inc(stat_free, 1)
            qk_norm(0)
            V.tensor_copy(xblk.rearrange("p t s -> p (t s)"), cst[:, C_EYE:C_EYE + BLK])
            dve.wait_ge(nblk_in, g * 16 + 16)
            settled(dve)
            for t in range(1, SUB):
                dve.drain()
                mul(prod[:, 0:t, 0:t], xblk[:, 0:t, 0:t].rearrange("p s j -> p j s"),
                    nblk[:, 0:t, t].unsqueeze(1).broadcast_to([P, t, t]))
                dve.drain()
                V.tensor_reduce(xblk[:, t, 0:t], prod[:, 0:t, 0:t], AX_X, ALU.add)
            dve.drain()
            V.tensor_copy(xblkt, xblk.rearrange("p t s -> p s t")).then_inc(blocks_done, 1)
            chunk_matrices("ak", ak_m)
            qk_norm(1)
            for n in range(2):
                V.tensor_copy(val[:, 4 * n:4 * n + 4, :], at_take(("v", n)).rearrange("p (a d) -> p a d", d=P)
                              ).then_inc(at_free, 1)
            def merged(m, h):
                return rk_take(("merge", m, h)).rearrange("p (c d) -> p c d", d=CH)

            for m, dst, mask in ((0, w_m, m1mask), (1, x_m, None), (2, xt_m, None), (3, w_m, m2mask), (4, xt_m, None)):
                for h in range(2):
                    part = dst[:, 8 * h:8 * h + 8, :]
                    if mask is not None:
                        V.tensor_tensor(part, merged(m, h), mask.unsqueeze(1).broadcast_to([P, 8, CH]),
                                        ALU.mult).then_inc(rk_free, 1)
                    else:
                        V.tensor_tensor(part, merged(m, h), part, ALU.add).then_inc(rk_free, 1)
            V.memset(s_t[:, 0, :], 0.0).then_inc(s_done, 1)

            def scores(qb, m):
                nh = qb // 4 + 1
                if qb == 0 and m == 0:
                    dve.wait_ge(bias_in, g * 16 + 16)
                for c in range(nh):
                    w = min(HALF, P * (qb + 1) - HALF * c)
                    off = SEQ - P - P * qb + HALF * c
                    bank = at_take(("s", qb, m, c))
                    settled(dve)
                    V.tensor_tensor_reduce(out=sc_b[:, m, HALF * c:HALF * c + w],
                                           in0=bank[:, 0:w], in1=bias_t[:, off:off + w],
                                           scale=1.0, scalar=-3e38, op0=ALU.add, op1=ALU.max,
                                           accum_out=mx[:, 2 * m + c:2 * m + c + 1]).then_inc(at_free, 1)

            def negate(qb):
                dve.drain()
                for m in range(2):
                    if qb < 4:
                        ins = V.tensor_scalar(nm[:, m:m + 1], mx[:, 2 * m:2 * m + 1], -1.0, None, ALU.mult)
                    else:
                        ins = V.tensor_scalar(nm[:, m:m + 1], mx[:, 2 * m:2 * m + 1], mx[:, 2 * m + 1:2 * m + 2],
                                              -1.0, ALU.max, ALU.mult)
                ins.then_inc(neg_done, 1)

            def weigh(qb):
                dve.wait_ge(exp_done, g * TT + (qb + 1))
                V.reciprocal(rl, ls)
                dve.drain()
                mul(c1, rl[:, 1:2], lam_neg)
                dve.drain()
                n = P * (qb + 1)
                V.tensor_scalar(sc_b[:, 1, 0:n], sc_b[:, 1, 0:n], c1, None, ALU.mult)

            def combine(qb):
                n = P * (qb + 1)
                dve.drain()
                stt(sc_b[:, 0, 0:n], sc_b[:, 0, 0:n], rl[:, 0:1], sc_b[:, 1, 0:n], ALU.mult, ALU.add).then_inc(attn_done, 1)

            def attn_out(qb):
                V.tensor_copy(o_b[:, P * qb:P * qb + P], at_take(("o", qb))[:, 0:P]).then_inc(at_free, 1)

            def y_take(h):
                dve.wait_ge(y_full, g * 2 + h + 1)
                V.tensor_copy(y_half[h], rk_ps[:, 1, :]).then_inc(y_out, 1)

            def y_centre(h):
                dve.wait_ge(stat_full, g * NST + (stat_no[f"ym{h}"] + 1))
                V.tensor_tensor(y_half[h], y_half[h], stat_ps[:], ALU.subtract).then_inc(stat_free, 1)

            def y_finish(h):
                dve.wait_ge(y_scaled, g * 2 + (h + 1))
                mul(y_half[h], y_half[h], y_nrm)
                dve.drain()
                affine(y_half[h], y_half[h], ln_wb[:, 0:1], ln_wb[:, 1:2])
                dve.drain()
                V.tensor_tensor(bonus[:, cols(h)], bonus[:, cols(h)], y_half[h], ALU.add)
                dve.drain()
                mul(bonus[:, cols(h)], bonus[:, cols(h)], ga_b[:, cols(h)]).then_inc(y_fin, 1)

            def gate_b(h):
                dve.wait_ge(proj_free, g * NPJ + (3 + 2 * 7 + h))
                sigmoid(gb_th[:, cols(h)])
                dve.drain()
                mul(gb_b[:, cols(h)], gb_b[:, cols(h)], gb_th[:, cols(h)])

            def gate_a():
                dve.wait_ge(proj_free, g * NPJ + (4 + 2 * 6))
                sigmoid(ga_th[:])
                dve.drain()
                mul(ga_b[:], ga_b[:], ga_th[:])

            def o_finish(h):
                dve.wait_ge(o_scaled, g * 2 + (h + 1))
                stt(o_b[:, cols(h)], o_b[:, cols(h)], shr[:, SUB_GS:SUB_GS + 1], o_nrm)
                dve.drain()
                mul(o_b[:, cols(h)], o_b[:, cols(h)], gb_b[:, cols(h)]).then_inc(o_fin, 1)

            for c in range(NCH):
                qb, odd = c // 2, c % 2
                dve.wait_ge(step_full, g * NSTEP + (3 * c + 1))
                V.tensor_copy(u0_t[:], rk_ps[:, 0, 0:CH]).then_inc(u0_done, 1)
                dve.drain()
                V.tensor_scalar(sp_t[:], s_t[:, c % 2, :], pc[:, c:c + 1], None, ALU.mult)
                if c == 8:
                    y_take(0)
                if not odd:
                    scores(qb, 0)
                else:
                    weigh(qb)
                dve.wait_ge(step_full, g * NSTEP + (3 * c + 2))
                V.tensor_copy(u_t[:, c % 2, :], rk_ps[:, 0, CH:2 * CH]).then_inc(u_done, 1)
                if not odd:
                    scores(qb, 1)
                    negate(qb)
                    if qb >= 1:
                        attn_out(qb - 1)
                else:
                    combine(qb)
                dve.wait_ge(step_full, g * NSTEP + (3 * c + 3))
                stt(s_t[:, (c + 1) % 2, :], rk_ps[:, 0, 2 * CH:3 * CH], pc[:, c:c + 1], sp_t[:], ALU.mult, ALU.add).then_inc(s_done, 1)
                if c == 8:
                    y_centre(0)
                if c == 1:
                    gate_a()
                if c == 9:
                    gate_b(0)
                if c == 15:
                    gate_b(1)
            V.tensor_copy(cur[:], prm_all[:, bass.ds(g + 1, 1), :].rearrange("p o n -> p (o n)"))
            dve.drain().then_inc(group_set, 1)
            y_take(1)
            y_centre(1)
            y_finish(0)
            attn_out(TT - 1)
            o_finish(0)
            y_finish(1)
            o_finish(1)

        for n, job in enumerate(TAIL):
            raw, high_part, low_part = split_parts(job)
            dve.wait_ge(tail_hi, n + 1)
            if job == ("w", 4):
                dve.drain()
            V.tensor_tensor(low_part, raw, high_part.bitcast(F32), ALU.subtract).then_inc(tail_split, 1)
        for t in range(TT):
            dve.wait_ge(res_in[t % 2], 16 * (t // 2 + 1))
            if t >= 2:
                dve.wait_ge(stored[t % 2], 16 * (t // 2))
            for h in range(2):
                n = 2 * t + h
                dve.wait_ge(out_full, n + 1)
                V.tensor_tensor(o_stage[:, t % 2, cols(h)], out_banks[n % 8], x_res[:, t % 2, cols(h)], ALU.add).then_inc(out_sum, 1)

    @block.tensor
    def _(pe):
        T = nc.tensor

        def three(bank, w_h, w_l, x_h, x_l, start, stop):
            T.matmul(bank, w_h, x_h, start=start, stop=False)
            T.matmul(bank, w_h, x_l, start=False, stop=False)
            return T.matmul(bank, w_l, x_h, start=False, stop=stop)

        def project(slot, h, ks, bank):
            for k in ks:
                w = slice(k * P, (k + 1) * P)
                ins = three(bank, w_hi[:, slot, w], w_lo[:, slot, w], hn_hi[:, k, cols(h)], hn_lo[:, k, cols(h)],
                            k == 0, k == KT - 1)
            return ins

        pe.wait_ge(c_loaded, 16 * 5)
        for n in range(2 * KT):
            h, k = n // KT, n % KT
            if n >= 3:
                pe.wait_ge(hn_done, n - 2)
            for i in range(4):
                t = 4 * h + i
                if k == 0:
                    pe.wait_ge(xn_done, t + 1)
                ins = T.transpose(at_ps[:, n % 3, i * P:(i + 1) * P], x_in[t][:, k * P:(k + 1) * P], ident)
            ins.then_inc(turned, 1)
            if k == KT - 1:
                pe.wait_ge(w_split, 1)
                pe.wait_ge(hn_done, KT * (h + 1))
                project(0, h, range(KT), proj_ps[:, h, :]).then_inc(proj_full, 1)

        with pe.Fori(0, GROUPS) as g:
            def proj_begin(j, h):
                pe.wait_ge(w_split, g * JOBS + (j + 2))
                pe.wait_ge(proj_free, g * NPJ + (2 * j + h + 1))

            def proj(j, h):
                proj_begin(j, h)
                project((j + 1) % 2, h, range(KT), proj_ps[:, h, :]).then_inc(proj_full, 1)

            def stat(name, lhs, rhs):
                if stat_bank(name) is stat_ps:
                    pe.wait_ge(stat_free, g * NST + (stat_no[name] + FROM))
                T.matmul(stat_bank(name)[:], lhs, rhs, start=True, stop=True).then_inc(stat_full, 1)

            def part(j, n):
                h, k = n // KT, n % KT
                if k == 0:
                    proj_begin(j, h)
                ins = project((j + 1) % 2, h, [k], proj_ps[:, h, :])
                if k == KT - 1:
                    ins.then_inc(proj_full, 1)

            proj(0, 0)
            proj(0, 1)
            pe.wait_ge(wlora_in, g * 16 + 16)
            pe.wait_ge(z_done, 1)
            stat("dec0", wlora[0:HEAD, :], z_t[0:HEAD, 0:HALF])
            for n in range(2 * KT):
                part(1, n)
                if n == 2:
                    stat("dec1", wlora[0:HEAD, :], z_t[0:HEAD, HALF:SEQ])
                if n == 4:
                    stat("icl0", wlora[HEAD:P, :], z_t[HEAD:P, 0:HALF])
                if n == 6:
                    stat("icl1", wlora[HEAD:P, :], z_t[HEAD:P, HALF:SEQ])
                if n == 9:
                    pe.wait_ge(kk_squared, g + 1)
                    stat("kk0", av64, sq[:, 0:HALF])
                if n == 12:
                    stat("kk1", av64, sq[:, HALF:SEQ])
            proj(2, 0)
            proj(2, 1)
            proj(3, 0)
            proj(3, 1)

            def rk_begin(job):
                n = rk_no[job]
                pe.wait_ge(rk_free, g * NRK + (max(n - 1, 0) + FROM))
                settled(pe)
                return rk_ps[:, n % 2, :]

            def at_begin(job):
                n = at_no[job]
                if n == 0:
                    pe.wait_ge(turn_free, g * NTURN + NTURN)
                elif n >= 3:
                    pe.wait_ge(*at_freed(g, AT_JOBS[n - 3]))
                return at_ps[:, n % 3, :]

            def turn(n):
                a, h = TURNS[n]
                src = (v_b, kk_b, k_b)[a]
                if n == 0:
                    pe.wait_ge(at_free, g * NAD + FROM)
                elif n >= 3:
                    pe.wait_ge(turn_free, g * NTURN + (n - 2))
                settled(pe)
                for c in range(8):
                    for hd in range(2):
                        r = rows(hd)
                        t0 = (8 * h + c) * CH
                        ins = T.matmul(at_ps[r, n % 3, c * CH:(c + 1) * CH], src[r, t0:t0 + CH],
                                       cst[r, C_ID + hd * HEAD:C_ID + hd * HEAD + HEAD], start=True, stop=True)
                ins.then_inc(turn_full, 1)

            def chunk_products(name, q):
                src = kk_b if name == "ab" else k_b
                bank = rk_begin((name, q))
                for i in range(4):
                    c = 4 * q + i
                    for hd in range(2):
                        r = rows(hd)
                        ins = T.matmul(bank[r, i * P:(i + 1) * P], src[r, c * CH:(c + 1) * CH],
                                       ar_t[r, c, :, :].rearrange("p x t -> p (x t)"), start=True, stop=True)
                ins.then_inc(rk_full, 1)

            def turn_values(n):
                bank = at_begin(("v", n))
                for i in range(4):
                    t = 4 * n + i
                    ins = T.transpose(bank[:, i * P:(i + 1) * P], v_b[:, t * P:(t + 1) * P], ident)
                ins.then_inc(at_full, 1)

            MERGES = ((0, ab_m[:, :, 0, :], x_m), (1, xt_m, w_m), (2, w_m, xt_m), (3, ab_m[:, :, 0, :], x_m),
                      (4, w_m, xt_m))

            def merge(n):
                m, lhs, rhs = MERGES[n // 2]
                h = n % 2
                bank = rk_begin(("merge", m, h))
                for c in range(8):
                    for hd in range(2):
                        r = rows(hd)
                        ins = T.matmul(bank[r, c * CH:(c + 1) * CH], lhs[r, 8 * h + c, :], rhs[r, 8 * h + c, :],
                                       start=True, stop=True)
                ins.then_inc(rk_full, 1)

            for n in range(2 * KT):
                part(4, n)
                if n in (3, 5):
                    h = (n - 3) // 2
                    stat(f"q{h}", av64, q_sqs[:, cols(h)])
                if n == 6:
                    pe.wait_ge(tildes, g + 1)
                if 6 <= n < 10:
                    chunk_products("ab", n - 6)
                if n in (10, 12):
                    h = (n - 10) // 2
                    stat(f"rk{h}", av64, sq[:, cols(h)])
                if n in (11, 13, 15):
                    turn((n - 11) // 2)
            for n in range(2 * KT):
                part(5, n)
                if n < 3:
                    turn(n + 3)
                if n in (5, 9):
                    h = (n - 5) // 4
                    stat(f"k{h}", av64, k_sqs[:, cols(h)])
                if n >= 12:
                    chunk_products("ak", n - 12)
            for n in range(2 * KT):
                part(6, n)
                if n == 1:
                    pe.wait_ge(proj_free, g * NPJ + (4 + 2 * 5))
                    pe.wait_ge(qk_done, g * 2 + 1)
                if n in (1, 2):
                    turn_values(n - 1)
                if n == 4:
                    pe.wait_ge(xblk_in, g * 256 + 256)
                if 4 <= n < 14:
                    merge(n - 4)

            def pair(col, terms, bank=0):
                settled(pe)
                for hd in range(2):
                    r = rows(hd)
                    for i, (lhs, rhs) in enumerate(terms):
                        ins = T.matmul(rk_ps[r, bank, col:col + CH], lhs[r], rhs[r], start=(i == 0),
                                       stop=(i == len(terms) - 1))
                return ins

            def scores(qb, m):
                for c in range(qb // 4 + 1):
                    w = min(HALF, P * (qb + 1) - HALF * c)
                    bank = at_begin(("s", qb, m, c))
                    T.matmul(bank[:, 0:w], q_z[:, m, qb * P:(qb + 1) * P], kq_b[:, HALF * c:HALF * c + w],
                             start=True, stop=True).then_inc(at_full, 1)

            def turn_attn(qb):
                pe.wait_ge(attn_done, g * TT + (qb + 1))
                for c in range(qb // 4 + 1):
                    bank = at_begin(("t", qb, c))
                    for i in range(min(4, qb + 1 - 4 * c)):
                        ins = T.transpose(bank[:, i * P:(i + 1) * P], sc_b[:, 0, (4 * c + i) * P:(4 * c + i + 1) * P], ident)
                    ins.then_inc(at_full, 1)

            def weigh_values(qb):
                pe.wait_ge(*at_freed(g, ("t", qb, qb // 4)))
                bank = at_begin(("o", qb))
                for k in range(qb + 1):
                    ins = T.matmul(bank[:, 0:P], val[:, k, :], attn_t[:, k, :], start=(k == 0), stop=(k == qb))
                ins.then_inc(at_full, 1)

            GATE_AT = [c for c, n in enumerate(GATE_PARTS) for _ in range(n)]

            pe.wait_ge(rk_free, g * NRK + (NRK + FROM))
            pe.wait_ge(qk_done, g * 2 + 2)
            for c in range(NCH):
                qb, odd = c // 2, c % 2
                pe.wait_ge(s_done, g * (NCH + 1) + (c + 1))
                pair(0, [(ak_m[:, c, 0, :], v_t[:, c, :]), (ar_t[:, c, 0, :], s_t[:, c % 2, :])]).then_inc(step_full, 1)
                if not odd:
                    if qb >= 1:
                        turn_attn(qb - 1)
                    scores(qb, 0)
                for n in range(2 * KT):
                    if GATE_AT[n] == c:
                        part(7, n)
                pe.wait_ge(u0_done, g * NCH + (c + 1))
                pair(CH, [(xt_m[:, c, :], u0_t[:])]).then_inc(step_full, 1)
                if not odd:
                    scores(qb, 1)
                    if qb >= 1:
                        weigh_values(qb - 1)
                pe.wait_ge(u_done, g * NCH + (c + 1))
                pair(2 * CH, [(k_t[:, c, :], v_t[:, c, :]), (b_t[:, c, :], u_t[:, c % 2, :])]).then_inc(step_full, 1)
                if c % 8 == 0 and c > 0:
                    pe.wait_ge(y_out, g * 2 + c // 8)
                ins = pair((c % 8) * CH, [(s_t[:, c % 2, :], ar_t[:, c, 1, :]), (u_t[:, c % 2, :], ab_m[:, c, 1, :]),
                                          (v_t[:, c, :], ak_m[:, c, 1, :])], bank=1)
                if c % 8 == 7:
                    ins.then_inc(y_full, 1)
                if c == 8:
                    stat("ym0", av64, y_half[0])
                if c == 10:
                    pe.wait_ge(y_sq, g * 2 + 1)
                    stat("yv0", av64, y_sqs)
                if c == 13:
                    pe.wait_ge(o_sq, g * 2 + 1)
                    stat("om0", av128, o_sqs)
            turn_attn(TT - 1)
            pe.wait_ge(y_out, g * 2 + 2)
            stat("ym1", av64, y_half[1])
            weigh_values(TT - 1)
            pe.wait_ge(y_sq, g * 2 + 2)
            stat("yv1", av64, y_sqs)
            pe.wait_ge(o_sq, g * 2 + 2)
            stat("om1", av128, o_sqs)

        pe.wait_ge(proj_free, GROUPS * NPJ + 2)
        pe.wait_ge(y_out, 2 * GROUPS)
        pe.wait_ge(at_free, GROUPS * NAD + FROM)
        pe.wait_ge(weights_out, GROUPS * NTA)
        pe.wait_ge(stat_free, GROUPS * NST + FROM)
        for outputs in (range(8), range(8, 12), range(12, 16)):
            for e in range(KT):
                if outputs[0] == 0:
                    if e == 0:
                        pe.wait_ge(pool_split, 2)
                    elif e == 1:
                        pe.wait_ge(pool_split, 3)
                    else:
                        pe.wait_ge(tail_split, tail_no["w", e] + 1)
                w_h, w_l = (wo_hi[:, e, :], wo_lo[:, e, :]) if e >= 2 else (w_hi[:, 1 - e, :], w_lo[:, 1 - e, :])
                for n in outputs:
                    if e == 0 and n >= 8:
                        pe.wait_ge(out_sum, n - 7)
                    t = slice((n // 2) * P, (n // 2 + 1) * P)
                    ins = three(out_banks[n % 8], hn_hi[:, e, t], hn_lo[:, e, t], w_h[:, cols(n % 2)],
                                w_l[:, cols(n % 2)], e == 0, e == KT - 1)
                    if e == KT - 1:
                        ins.then_inc(out_full, 1)


def host_constants():
    p = np.arange(P)
    cst = np.zeros((P, C_WIDTH), np.float32)
    cst[:, C_ID:C_ID + P] = np.eye(P)
    cst[:, C_AV64:C_AV64 + P] = (p[:, None] // HEAD == p[None, :] // HEAD) / HEAD
    cst[:, C_AV128:C_AV128 + P] = 1.0 / P
    s, t = (p % CH)[:, None], np.arange(CH)[None, :]
    cst[:, C_AMASK:C_AMASK + CH] = s < t
    cst[:, C_AMASK + CH:C_AMASK + 2 * CH] = s <= t
    row, col = s, t
    cst[:, C_M1:C_M1 + CH] = ((row // 32) == (col // 32)) & ((row // 16) % 2 == 1) & ((col // 16) % 2 == 0)
    cst[:, C_M2:C_M2 + CH] = (row >= 32) & (col < 32)
    cst[:, C_EYE:C_EYE + BLK] = np.eye(SUB).reshape(1, BLK)
    dist = p[:, None] + (SEQ - P) - np.arange(SEQ)[None, :]
    slopes = [2.0 ** (-8.0 * (h + 1) / GROUPS) for h in range(GROUPS)]
    alibi = np.stack([np.where(dist >= 0, -sl * dist, -1e30) for sl in slopes]).astype(np.float32)
    return cst, alibi


def kernel(x, norm_g, w_in, shift_mu, w0, w_decay_up, a0, w_iclr_up, k_k, k_a, r_k, ln_x_w, ln_x_b,
           q_norm_g, k_norm_g, lambda_q1, lambda_k1, lambda_q2, lambda_k2, subln_g, w_out):
    import concourse.bacc as _bacc
    from concourse.bass_utils import run_bass_kernel_spmd as _run

    A = np.asarray
    W = GROUPS * P

    def tiles(w):
        w = A(w)
        return w.reshape(KT, P, w.shape[1] // P, P).transpose(2, 1, 0, 3).reshape(-1, P, SEQ)

    wt = tiles(A(w_in)[0])
    order = [12]
    for g in range(GROUPS):
        order += [4 + g, g, 8 + g, 17 + g, 21 + g, 25 + g, 13 + g, 29 + g]
    w_all = np.ascontiguousarray(np.concatenate([wt[order], A(w_out)[0].reshape(KT, P, D_MODEL)[mix_order()]]))

    def per_group(v):
        return A(v).reshape(GROUPS, P).T

    mu = A(shift_mu)[0]
    prm = np.ascontiguousarray(np.stack([per_group(v) for v in (
        mu[0:W], mu[W:2 * W], mu[2 * W:3 * W], A(w0)[0], A(a0)[0], A(k_k)[0], A(k_a)[0], A(r_k)[0],
        A(ln_x_w)[0], A(ln_x_b)[0])], axis=2))
    qg, kg = A(q_norm_g)[0], A(k_norm_g)[0]
    shared = np.ascontiguousarray(np.stack([mu[3 * W:], np.tile(qg, 2), np.tile(kg, 2), A(subln_g)[0]], axis=1))
    lam_in = np.ascontiguousarray(np.broadcast_to(
        np.stack([A(lambda_q1)[0], A(lambda_q2)[0], A(lambda_k1)[0], A(lambda_k2)[0]])[None], (P, 4, HEAD)))
    ng = np.ascontiguousarray(A(norm_g)[0].reshape(KT, P).T)
    w_lora = np.concatenate([A(w_decay_up)[0], A(w_iclr_up)[0]]).reshape(P, GROUPS, P).transpose(1, 0, 2)
    w_lora = np.ascontiguousarray(np.concatenate([w_lora, w_lora[:1]]))
    cst, alibi = host_constants()
    arrays = {"x": np.ascontiguousarray(A(x)[0]), "w_all": w_all, "prm": prm, "shared": shared, "lam_in": lam_in,
              "norm_g": ng, "w_lora": w_lora, "consts": cst, "alibi": alibi}
    nc = _bacc.Bacc("TRN2", target_bir_lowering=False, num_devices=1)
    args = [nc.dram_tensor(n, a.shape, F32, kind="ExternalInput").ap() for n, a in arrays.items()]
    args.append(nc.dram_tensor("out", (SEQ, D_MODEL), F32, kind="ExternalOutput").ap())
    for n, s in (("mixed", (KT, P, SEQ)), ("nblk_d", (8, NCH, SUB, SUB)), ("xblk_d", (2, 8, NCH, SUB, SUB))):
        args.append(nc.dram_tensor(n, s, F32, kind="Internal").ap())
    with ExitStack() as ctx:
        build(nc, ctx, *args)
    r = _run(nc, [arrays], core_ids=[0])
    return r.results[0]["out"].reshape(1, SEQ, D_MODEL)
```
